# Optimizing a Trainium2 kernel written in Bass

```python
import math
import jax, jax.numpy as jnp
from jax import lax
import numpy as np

D_MODEL = 1024
BATCH = 1
SEQ = 256
DEPTH = 1

EPS = 1e-6
HG_HEADS = 8
HG_KDIM = 128
HG_VDIM = 128
HG_CHUNK = 64
HG_WIDTH_K = HG_HEADS * HG_KDIM
HG_WIDTH_V = HG_HEADS * HG_VDIM
MLA_HEADS = 8
MLA_Q_RANK = 384
MLA_KV_RANK = 256
MLA_NOPE = 128
MLA_ROPE = 64
MLA_VDIM = 128
MLA_QK_DIM = MLA_NOPE + MLA_ROPE
ROPE_THETA = 10000.0
Q_BLOCK = 128
N_BRANCH = 2
IN_SPLITS = (HG_WIDTH_K, HG_WIDTH_K, HG_WIDTH_V, HG_WIDTH_V, MLA_Q_RANK, MLA_KV_RANK, MLA_ROPE, D_MODEL, D_MODEL)
IN_COLS = sum(IN_SPLITS)
N_GROUPS = 8
EXPERTS_PER_GROUP = 8
N_EXPERTS = N_GROUPS * EXPERTS_PER_GROUP
TOP_K_IN_GROUP = 2
EXPERT_FF = 512
MOE_BLOCK = 128


def rmsnorm(x, w):
    xf = x.astype(jnp.float32)
    y = xf * lax.rsqrt(jnp.mean(xf * xf, axis=-1, keepdims=True) + EPS)
    return (y * w.astype(jnp.float32)).astype(x.dtype)

def apply_rope(x, cos, sin):
    x1, x2 = jnp.split(x.astype(jnp.float32), 2, axis=-1)
    return jnp.concatenate([x1 * cos - x2 * sin, x2 * cos + x1 * sin], axis=-1).astype(x.dtype)

def hgrn2_mixer(q_raw, f_raw, i_raw, g_raw, lb, out_norm_w):
    B, S, _ = q_raw.shape
    n = S // HG_CHUNK
    f32 = jnp.float32
    q = jax.nn.silu(q_raw.astype(f32)) * (HG_KDIM ** -0.5)
    lbf = lb.astype(f32)
    fg = lbf + (1.0 - lbf) * jax.nn.sigmoid(f_raw.astype(f32))
    k = 1.0 - fg
    logf = jnp.log(fg)
    v = i_raw.astype(f32)

    def to_chunks(t, d):
        return t.reshape(B, n, HG_CHUNK, HG_HEADS, d).transpose(1, 0, 3, 2, 4)

    qc, kc, lfc = to_chunks(q, HG_KDIM), to_chunks(k, HG_KDIM), to_chunks(logf, HG_KDIM)
    vc = to_chunks(v, HG_VDIM)
    causal = jnp.tril(jnp.ones((HG_CHUNK, HG_CHUNK), dtype=bool))

    def step(state, inp):
        qt, kt, lft, vt = inp
        bcum = jnp.cumsum(lft, axis=2)
        diff = bcum[:, :, :, None, :] - bcum[:, :, None, :, :]
        decay = jnp.exp(jnp.where(causal[None, None, :, :, None], diff, -jnp.inf))
        attn = jnp.sum(qt[:, :, :, None, :] * kt[:, :, None, :, :] * decay, axis=-1)
        o = jnp.einsum('bhts,bhsv->bhtv', attn, vt) + \
            jnp.einsum('bhtk,bhkv->bhtv', qt * jnp.exp(bcum), state)
        b_last = bcum[:, :, -1]
        k_dec = kt * jnp.exp(b_last[:, :, None, :] - bcum)
        state = jnp.exp(b_last)[..., None] * state + jnp.einsum('bhsk,bhsv->bhkv', k_dec, vt)
        return state, o

    s0 = jnp.zeros((B, HG_HEADS, HG_KDIM, HG_VDIM), f32)
    _, o = lax.scan(step, s0, (qc, kc, lfc, vc))
    o = o.transpose(1, 0, 3, 2, 4).reshape(B, S, HG_HEADS, HG_VDIM)
    o = rmsnorm(o, out_norm_w).reshape(B, S, HG_WIDTH_V)
    g = g_raw.astype(f32)
    return o * jax.nn.silu(g)

def mla_mixer(c_q, c_kv, k_rope_raw, positions, q_norm_w, w_uq, kv_norm_w, w_ukv):
    B, S, _ = c_q.shape
    half = MLA_ROPE // 2
    inv_freq = ROPE_THETA ** (-jnp.arange(half, dtype=jnp.float32) / half)
    ang = positions.astype(jnp.float32)[..., None] * inv_freq
    cos, sin = jnp.cos(ang), jnp.sin(ang)

    q = (rmsnorm(c_q, q_norm_w) @ w_uq).reshape(B, S, MLA_HEADS, MLA_QK_DIM)
    q_nope, q_pe = q[..., :MLA_NOPE], q[..., MLA_NOPE:]
    q_pe = apply_rope(q_pe, cos[:, :, None, :], sin[:, :, None, :])
    kv = (rmsnorm(c_kv, kv_norm_w) @ w_ukv).reshape(B, S, MLA_HEADS, MLA_NOPE + MLA_VDIM)
    k_nope, v = kv[..., :MLA_NOPE], kv[..., MLA_NOPE:]
    k_pe = apply_rope(k_rope_raw, cos, sin)
    k = jnp.concatenate([k_nope, jnp.broadcast_to(k_pe[:, :, None, :], (B, S, MLA_HEADS, MLA_ROPE))], axis=-1)
    qf = jnp.concatenate([q_nope, q_pe], axis=-1) * (MLA_QK_DIM ** -0.5)

    nq = S // Q_BLOCK
    qb = qf.reshape(B, nq, Q_BLOCK, MLA_HEADS, MLA_QK_DIM).transpose(1, 0, 3, 2, 4)
    kpos = jnp.arange(S)

    def attend(args):
        qblk, blk = args
        s = jnp.einsum('bhqd,bkhd->bhqk', qblk, k, preferred_element_type=jnp.float32)
        qpos = blk * Q_BLOCK + jnp.arange(Q_BLOCK)
        s = jnp.where(kpos[None, :] <= qpos[:, None], s, -jnp.inf)
        p = jax.nn.softmax(s, axis=-1)
        return jnp.einsum('bhqk,bkhd->bqhd', p.astype(v.dtype), v)

    o = lax.map(attend, (qb, jnp.arange(nq)))
    return o.transpose(1, 0, 2, 3, 4).reshape(B, S, MLA_HEADS * MLA_VDIM)

def hierarchical_moe(h, w_group, b_group, w_expert, b_expert, w1, w3, w2):
    B, S, D = h.shape
    T = B * S
    xt = h.reshape(T, D)
    g_prob = jax.nn.softmax((xt @ w_group).astype(jnp.float32) + b_group.astype(jnp.float32), axis=-1)
    g_w, g_idx = lax.top_k(g_prob, 1)
    e_logits = ((xt @ w_expert).astype(jnp.float32) + b_expert.astype(jnp.float32)).reshape(T, N_GROUPS, EXPERTS_PER_GROUP)
    e_sel = jnp.take_along_axis(e_logits, g_idx[:, :, None], axis=1)[:, 0]
    e_prob = jax.nn.softmax(e_sel, axis=-1)
    e_w, e_idx = lax.top_k(e_prob, TOP_K_IN_GROUP)
    e_w = e_w / jnp.sum(e_w, axis=-1, keepdims=True)
    weights = g_w * e_w
    expert_ids = g_idx * EXPERTS_PER_GROUP + e_idx

    A = T * TOP_K_IN_GROUP
    flat_e = expert_ids.reshape(A)
    flat_t = jnp.repeat(jnp.arange(T, dtype=jnp.int32), TOP_K_IN_GROUP)
    flat_w = weights.reshape(A)
    order = jnp.argsort(flat_e)
    se, st, sw = flat_e[order], flat_t[order], flat_w[order]
    counts = jax.ops.segment_sum(jnp.ones_like(se), se, num_segments=N_EXPERTS)
    starts = jnp.cumsum(counts) - counts
    padded = (counts + MOE_BLOCK - 1) // MOE_BLOCK * MOE_BLOCK
    pends = jnp.cumsum(padded)
    pstarts = pends - padded
    dest = pstarts[se] + (jnp.arange(A, dtype=se.dtype) - starts[se])
    n_blocks = A // MOE_BLOCK + N_EXPERTS
    cap = n_blocks * MOE_BLOCK
    tok_buf = jnp.full((cap,), T, dtype=jnp.int32).at[dest].set(st)
    w_buf = jnp.zeros((cap,), jnp.float32).at[dest].set(sw)
    block_start = jnp.arange(n_blocks, dtype=pends.dtype) * MOE_BLOCK
    block_expert = jnp.minimum(jnp.searchsorted(pends, block_start, side='right'), N_EXPERTS - 1)
    x_pad = jnp.concatenate([xt, jnp.zeros((1, D), xt.dtype)], axis=0)

    def run_block(args):
        toks, wts, e = args
        xb = x_pad[toks]
        hid = jax.nn.silu(xb @ w1[e]) * (xb @ w3[e])
        return (hid @ w2[e]) * wts[:, None].astype(xb.dtype)

    yb = lax.map(run_block, (tok_buf.reshape(n_blocks, MOE_BLOCK), w_buf.reshape(n_blocks, MOE_BLOCK), block_expert))
    out = jax.ops.segment_sum(yb.reshape(cap, D), tok_buf, num_segments=T + 1)[:T]
    return out.reshape(B, S, D)

def first_inputs(seed: int = 0) -> dict:
    key = jax.random.key(seed)
    ks = jax.random.split(key, 24)
    f32 = jnp.float32
    nrm = lambda k, shape, scale: jax.random.normal(k, shape, f32) * scale
    gain = lambda k, shape: 1.0 + 0.02 * jax.random.normal(k, shape, f32)
    x = jax.random.normal(ks[0], (BATCH, SEQ, D_MODEL), f32)
    offsets = jax.random.randint(ks[1], (BATCH, 1), 0, 4096, dtype=jnp.int32)
    positions = offsets + jnp.arange(SEQ, dtype=jnp.int32)[None, :]
    return {
        "x": x,
        "positions": positions,
        "attn_norm_w": gain(ks[2], (DEPTH, D_MODEL)),
        "w_in": nrm(ks[3], (DEPTH, D_MODEL, IN_COLS), D_MODEL ** -0.5),
        "hg_lower_bound": nrm(ks[4], (DEPTH + 1, HG_WIDTH_K), 0.5),
        "hg_out_norm_w": gain(ks[5], (DEPTH, HG_VDIM)),
        "mla_q_norm_w": gain(ks[6], (DEPTH, MLA_Q_RANK)),
        "mla_w_uq": nrm(ks[7], (DEPTH, MLA_Q_RANK, MLA_HEADS * MLA_QK_DIM), MLA_Q_RANK ** -0.5),
        "mla_kv_norm_w": gain(ks[8], (DEPTH, MLA_KV_RANK)),
        "mla_w_ukv": nrm(ks[9], (DEPTH, MLA_KV_RANK, MLA_HEADS * (MLA_NOPE + MLA_VDIM)), MLA_KV_RANK ** -0.5),
        "w_branch_hgrn": nrm(ks[10], (DEPTH, HG_WIDTH_V, D_MODEL), HG_WIDTH_V ** -0.5),
        "w_branch_mla": nrm(ks[11], (DEPTH, MLA_HEADS * MLA_VDIM, D_MODEL), (MLA_HEADS * MLA_VDIM) ** -0.5),
        "w_out": nrm(ks[12], (DEPTH, D_MODEL, D_MODEL), D_MODEL ** -0.5),
        "ffn_norm_w": gain(ks[13], (DEPTH, D_MODEL)),
        "router_group_w": nrm(ks[14], (DEPTH, D_MODEL, N_GROUPS), D_MODEL ** -0.5),
        "router_group_b": nrm(ks[15], (DEPTH, N_GROUPS), 0.01),
        "router_expert_w": nrm(ks[16], (DEPTH, D_MODEL, N_EXPERTS), D_MODEL ** -0.5),
        "router_expert_b": nrm(ks[17], (DEPTH, N_EXPERTS), 0.01),
        "expert_w1": nrm(ks[18], (DEPTH, N_EXPERTS, D_MODEL, EXPERT_FF), D_MODEL ** -0.5),
        "expert_w3": nrm(ks[19], (DEPTH, N_EXPERTS, D_MODEL, EXPERT_FF), D_MODEL ** -0.5),
        "expert_w2": nrm(ks[20], (DEPTH, N_EXPERTS, EXPERT_FF, D_MODEL), EXPERT_FF ** -0.5),
        "final_norm_w": gain(ks[21], (D_MODEL,)),
    }

def first_block(x, positions, attn_norm_w, w_in, hg_lower_bound, hg_out_norm_w, mla_q_norm_w, mla_w_uq,
              mla_kv_norm_w, mla_w_ukv, w_branch_hgrn, w_branch_mla, w_out, ffn_norm_w, router_group_w,
              router_group_b, router_expert_w, router_expert_b, expert_w1, expert_w3, expert_w2, final_norm_w):
    split_idx = [int(v) for v in np.cumsum(IN_SPLITS)[:-1]]
    lb_all = jnp.cumsum(jax.nn.softmax(hg_lower_bound.astype(jnp.float32), axis=0), axis=0)
    for l in range(DEPTH):
        h = rmsnorm(x, attn_norm_w[l])
        z = h @ w_in[l]
        hq, hf, hi, hg, cq, ckv, kr, gate_a, gate_b = jnp.split(z, split_idx, axis=-1)
        o_a = hgrn2_mixer(hq, hf, hi, hg, lb_all[l], hg_out_norm_w[l]).astype(x.dtype)
        o_b = mla_mixer(cq, ckv, kr, positions, mla_q_norm_w[l], mla_w_uq[l], mla_kv_norm_w[l], mla_w_ukv[l])
        y = jax.nn.sigmoid(gate_a) * (o_a @ w_branch_hgrn[l]) + jax.nn.sigmoid(gate_b) * (o_b @ w_branch_mla[l])
        x = x + y @ w_out[l]
        h = rmsnorm(x, ffn_norm_w[l])
        x = x + hierarchical_moe(h, router_group_w[l], router_group_b[l], router_expert_w[l], router_expert_b[l],
                                 expert_w1[l], expert_w3[l], expert_w2[l])
    return rmsnorm(x, final_norm_w)


HEAD_DIM = 64
MOBA_HEADS = 8
MOBA_BLOCK = 256
MOBA_TOPK = 3
MOBA_Q_CHUNK = 8
DSA_HEADS = 8
DSA_TOPK = 256
DSA_Q_CHUNK = 16
IDX_HEADS = 8
IDX_DIM = 64
MEM_LEN = 256
X_HEADS = 4
X_HEAD_DIM = 128
RMS_EPS = 1e-6
N_BRANCH_2 = 3
MOBA_W = MOBA_HEADS * HEAD_DIM
DSA_W = DSA_HEADS * HEAD_DIM
X_W = X_HEADS * X_HEAD_DIM
IN_SIZES = (MOBA_W, MOBA_W, MOBA_W, MOBA_W, DSA_W, DSA_W, DSA_W, DSA_W,
            IDX_HEADS * IDX_DIM, IDX_DIM, IDX_HEADS, X_W, X_W, N_BRANCH_2 * D_MODEL)
IN_WIDTH = 4 * MOBA_W + 4 * DSA_W + IDX_HEADS * IDX_DIM + IDX_DIM + IDX_HEADS + 2 * X_W + N_BRANCH_2 * D_MODEL


NEG_INF = -jnp.inf

def rmsnorm_2(x, g):
    xf = x.astype(jnp.float32)
    y = xf * lax.rsqrt(jnp.mean(xf * xf, axis=-1, keepdims=True) + RMS_EPS)
    return (y * g.astype(jnp.float32)).astype(x.dtype)

def rope(x, pos):
    d = x.shape[-1]
    half = d // 2
    inv = jnp.power(ROPE_THETA, -jnp.arange(half, dtype=jnp.float32) * 2.0 / d)
    ang = pos.astype(jnp.float32)[:, None] * inv[None, :]
    cos = jnp.cos(ang)[None, :, None, :]
    sin = jnp.sin(ang)[None, :, None, :]
    xf = x.astype(jnp.float32)
    x1, x2 = xf[..., :half], xf[..., half:]
    return jnp.concatenate([x1 * cos - x2 * sin, x2 * cos + x1 * sin], axis=-1).astype(x.dtype)

def moba_attention(q, k, v):
    B, S, H, D = q.shape
    nb = -(-S // MOBA_BLOCK)
    sp = nb * MOBA_BLOCK
    padw = ((0, 0), (0, sp - S), (0, 0), (0, 0))
    qp, kp, vp = jnp.pad(q, padw), jnp.pad(k, padw), jnp.pad(v, padw)
    scale = D ** -0.5
    kbh = kp.reshape(B, nb, MOBA_BLOCK, H, D).transpose(0, 3, 1, 2, 4)
    vbh = vp.reshape(B, nb, MOBA_BLOCK, H, D).transpose(0, 3, 1, 2, 4)
    kmean = jnp.mean(kbh.astype(jnp.float32), axis=3)
    gate = jnp.einsum('bshd,bhnd->bshn', qp.astype(jnp.float32), kmean)
    qblk = jnp.arange(sp) // MOBA_BLOCK
    past = jnp.arange(nb)[None, :] < qblk[:, None]
    gate = jnp.where(past[None, :, None, :], gate, NEG_INF)
    n_sel = max(min(MOBA_TOPK, nb - 1), 1)
    top_val, top_idx = lax.top_k(gate, n_sel)
    top_ok = jnp.isfinite(top_val)
    nc = sp // MOBA_Q_CHUNK
    b_ix = jnp.arange(B)[:, None, None, None]
    h_ix = jnp.arange(H)[None, None, :, None]

    def to_chunks(a):
        return a.reshape((B, nc, MOBA_Q_CHUNK) + a.shape[2:]).swapaxes(0, 1)

    def step(args):
        ci, q_c, idx_c, ok_c = args
        t0 = ci * MOBA_Q_CHUNK
        blk_start = (t0 // MOBA_BLOCK) * MOBA_BLOCK
        k_own = lax.dynamic_slice_in_dim(kp, blk_start, MOBA_BLOCK, axis=1)
        v_own = lax.dynamic_slice_in_dim(vp, blk_start, MOBA_BLOCK, axis=1)
        qpos = t0 + jnp.arange(MOBA_Q_CHUNK)
        kpos = blk_start + jnp.arange(MOBA_BLOCK)
        s_own = jnp.einsum('bqhd,bkhd->bhqk', q_c, k_own).astype(jnp.float32) * scale
        s_own = jnp.where((kpos[None, :] <= qpos[:, None])[None, None], s_own, NEG_INF)
        k_sel = kbh[b_ix, h_ix, idx_c]
        v_sel = vbh[b_ix, h_ix, idx_c]
        s_past = jnp.einsum('bqhd,bqhnkd->bhqnk', q_c, k_sel).astype(jnp.float32) * scale
        s_past = jnp.where(ok_c.transpose(0, 2, 1, 3)[..., None], s_past, NEG_INF)
        n_past = n_sel * MOBA_BLOCK
        s_all = jnp.concatenate([s_past.reshape(B, H, MOBA_Q_CHUNK, n_past), s_own], axis=-1)
        p = jax.nn.softmax(s_all, axis=-1).astype(q.dtype)
        p_past = p[..., :n_past].reshape(B, H, MOBA_Q_CHUNK, n_sel, MOBA_BLOCK)
        p_own = p[..., n_past:]
        return (jnp.einsum('bhqnk,bqhnkd->bqhd', p_past, v_sel)
                + jnp.einsum('bhqk,bkhd->bqhd', p_own, v_own))

    outs = lax.map(step, (jnp.arange(nc), to_chunks(qp), to_chunks(top_idx), to_chunks(top_ok)))
    return outs.swapaxes(0, 1).reshape(B, sp, H, D)[:, :S]

def dsa_attention(q, k, v, iq, ik, iw):
    B, S, H, D = q.shape
    k_top = min(DSA_TOPK, S // 4)
    nc = S // DSA_Q_CHUNK
    scale = D ** -0.5
    iscale = IDX_DIM ** -0.5
    wscale = IDX_HEADS ** -0.5
    b_ix = jnp.arange(B)[:, None, None]
    kpos = jnp.arange(S)

    def to_chunks(a):
        return a.reshape((B, nc, DSA_Q_CHUNK) + a.shape[2:]).swapaxes(0, 1)

    def step(args):
        ci, q_c, iq_c, iw_c = args
        qpos = ci * DSA_Q_CHUNK + jnp.arange(DSA_Q_CHUNK)
        logits = jnp.einsum('bqgd,bsd->bqgs', iq_c, ik).astype(jnp.float32) * iscale
        score = jnp.einsum('bqgs,bqg->bqs', jax.nn.relu(logits), iw_c.astype(jnp.float32) * wscale)
        score = jnp.where((kpos[None, :] <= qpos[:, None])[None], score, NEG_INF)
        top_val, top_idx = lax.top_k(score, k_top)
        ok = jnp.isfinite(top_val)
        k_sel = k[b_ix, top_idx]
        v_sel = v[b_ix, top_idx]
        s = jnp.einsum('bqhd,bqkhd->bhqk', q_c, k_sel).astype(jnp.float32) * scale
        s = jnp.where(ok[:, None], s, NEG_INF)
        p = jax.nn.softmax(s, axis=-1).astype(q.dtype)
        return jnp.einsum('bhqk,bqkhd->bqhd', p, v_sel)

    outs = lax.map(step, (jnp.arange(nc), to_chunks(q), to_chunks(iq), to_chunks(iw)))
    return outs.swapaxes(0, 1).reshape(B, S, H, D)

def cross_attention(q, mk, mv):
    scale = q.shape[-1] ** -0.5
    s = jnp.einsum('bshd,bmhd->bhsm', q, mk).astype(jnp.float32) * scale
    p = jax.nn.softmax(s, axis=-1).astype(q.dtype)
    return jnp.einsum('bhsm,bmhd->bshd', p, mv)

def hybrid_layer(x, mem, g_in, w_in, b_merge, g_mem, w_mem_kv, w_up_moba, w_up_dsa, w_up_cross, w_out):
    B, S, _ = x.shape
    pos = jnp.arange(S)
    h = rmsnorm_2(x, g_in)
    z = h @ w_in
    offs = np.cumsum(IN_SIZES)[:-1].tolist()
    (mq, mk, mv, mg, dq, dk, dv, dg, iq, ik, iw, xq, xg, glog) = jnp.split(z, offs, axis=-1)
    heads = lambda a, n, d: a.reshape(B, S, n, d)
    mq = rope(heads(mq, MOBA_HEADS, HEAD_DIM), pos)
    mk = rope(heads(mk, MOBA_HEADS, HEAD_DIM), pos)
    ya = moba_attention(mq, mk, heads(mv, MOBA_HEADS, HEAD_DIM)).reshape(B, S, MOBA_W)
    ya = (ya * jax.nn.silu(mg)) @ w_up_moba
    dq = rope(heads(dq, DSA_HEADS, HEAD_DIM), pos)
    dk = rope(heads(dk, DSA_HEADS, HEAD_DIM), pos)
    iq = rope(heads(iq, IDX_HEADS, IDX_DIM), pos)
    ik = rope(ik[:, :, None, :], pos)[:, :, 0, :]
    yb = dsa_attention(dq, dk, heads(dv, DSA_HEADS, HEAD_DIM), iq, ik, iw).reshape(B, S, DSA_W)
    yb = (yb * jax.nn.silu(dg)) @ w_up_dsa
    M = mem.shape[1]
    kv = rmsnorm_2(mem, g_mem) @ w_mem_kv
    xk = kv[..., :X_W].reshape(B, M, X_HEADS, X_HEAD_DIM)
    xv = kv[..., X_W:].reshape(B, M, X_HEADS, X_HEAD_DIM)
    yc = cross_attention(heads(xq, X_HEADS, X_HEAD_DIM), xk, xv).reshape(B, S, X_W)
    yc = (yc * jax.nn.silu(xg)) @ w_up_cross
    gates = jax.nn.sigmoid(glog + b_merge).reshape(B, S, N_BRANCH_2, D_MODEL)
    u = gates[:, :, 0] * ya + gates[:, :, 1] * yb + gates[:, :, 2] * yc
    return x + u @ w_out

def second_inputs(seed: int = 0) -> dict:
    key = jax.random.key(seed)
    ks = jax.random.split(key, 12)
    f32 = jnp.float32
    nrm = lambda k, shape, s: jax.random.normal(k, shape, f32) * s
    return {
        'x': nrm(ks[0], (BATCH, SEQ, D_MODEL), 1.0),
        'mem': nrm(ks[1], (BATCH, MEM_LEN, D_MODEL), 1.0),
        'g_in': 1.0 + nrm(ks[2], (DEPTH, D_MODEL), 0.02),
        'w_in': nrm(ks[3], (DEPTH, D_MODEL, IN_WIDTH), D_MODEL ** -0.5),
        'b_merge': nrm(ks[4], (DEPTH, N_BRANCH_2 * D_MODEL), 0.1),
        'g_mem': 1.0 + nrm(ks[5], (DEPTH, D_MODEL), 0.02),
        'w_mem_kv': nrm(ks[6], (DEPTH, D_MODEL, 2 * X_W), D_MODEL ** -0.5),
        'w_up_moba': nrm(ks[7], (DEPTH, MOBA_W, D_MODEL), MOBA_W ** -0.5),
        'w_up_dsa': nrm(ks[8], (DEPTH, DSA_W, D_MODEL), DSA_W ** -0.5),
        'w_up_cross': nrm(ks[9], (DEPTH, X_W, D_MODEL), X_W ** -0.5),
        'w_out': nrm(ks[10], (DEPTH, D_MODEL, D_MODEL), D_MODEL ** -0.5),
        'g_final': 1.0 + nrm(ks[11], (D_MODEL,), 0.02),
    }

def second_block(x, mem, g_in, w_in, b_merge, g_mem, w_mem_kv, w_up_moba, w_up_dsa, w_up_cross, w_out, g_final):
    for l in range(DEPTH):
        x = hybrid_layer(x, mem, g_in[l], w_in[l], b_merge[l], g_mem[l], w_mem_kv[l],
                         w_up_moba[l], w_up_dsa[l], w_up_cross[l], w_out[l])
    return rmsnorm_2(x, g_final)


def setup_inputs(seed=0):
    out = dict(first_inputs(seed))
    for name, value in second_inputs(seed + 1).items():
        if name != "x":
            out[name + "_2"] = value
    return out


def reference(
    x, positions, attn_norm_w, w_in, hg_lower_bound, hg_out_norm_w, mla_q_norm_w, mla_w_uq,
    mla_kv_norm_w, mla_w_ukv, w_branch_hgrn, w_branch_mla, w_out, ffn_norm_w, router_group_w,
    router_group_b, router_expert_w, router_expert_b, expert_w1, expert_w3, expert_w2,
    final_norm_w, mem_2, g_in_2, w_in_2, b_merge_2, g_mem_2, w_mem_kv_2, w_up_moba_2,
    w_up_dsa_2, w_up_cross_2, w_out_2, g_final_2,
):
    x = first_block(
        x, positions, attn_norm_w, w_in, hg_lower_bound, hg_out_norm_w, mla_q_norm_w, mla_w_uq,
        mla_kv_norm_w, mla_w_ukv, w_branch_hgrn, w_branch_mla, w_out, ffn_norm_w,
        router_group_w, router_group_b, router_expert_w, router_expert_b, expert_w1, expert_w3,
        expert_w2, final_norm_w,
    )
    return second_block(
        x, mem_2, g_in_2, w_in_2, b_merge_2, g_mem_2, w_mem_kv_2, w_up_moba_2, w_up_dsa_2,
        w_up_cross_2, w_out_2, g_final_2,
    )


_drawn_inputs = setup_inputs


def setup_inputs(seed=0):
    import zlib

    import numpy as np

    out = dict(_drawn_inputs(seed))
    spreads = {}
    factors = {'hg_out_norm_w': 3.606,
     'mla_q_norm_w': 8.0,
     'mla_kv_norm_w': 6.854,
     'router_group_b': 3.869,
     'router_expert_b': 8.0,
     'g_in_2': 5.936,
     'b_merge_2': 8.0,
     'g_mem_2': 8.0}
    for name, (base, spread) in spreads.items():
        noise = np.random.default_rng([zlib.crc32(name.encode()), seed]).standard_normal(out[name].shape)
        drawn = base * np.exp(spread * noise) if base else spread * noise
        out[name] = __import__('jax').numpy.asarray(drawn.astype(out[name].dtype))
    for name, factor in factors.items():
        out[name] = (out[name] * factor).astype(out[name].dtype)
    return out
```

```python
from contextlib import ExitStack

import numpy as np
import concourse.bass as bass
from concourse import mybir

F32 = mybir.dt.float32
I32 = mybir.dt.int32
U32 = mybir.dt.uint32
ALU = mybir.AluOpType
ACT = mybir.ActivationFunctionType
AX = mybir.AxisListType

P = 128
S = 256
NT = S // P
D = 1024
KC = D // P
EPS = 1e-6
NEG = -1e30
USED = -3e38
SLOTS = 4
SLOT = 4096
HH = 8
XH = 4
HG_SCALE = 128 ** -0.5
MLA_Q, MLA_KV, MLA_ROPE = 384, 256, 64
MLA_SCALE = 192 ** -0.5
NG, NE_G, FF = 8, 8, 512
NEXP = NG * NE_G
CAP = 32
EG = 4
GROUPS = NEXP // EG
SEL = 128
TOPK = 64

LEVELS = [1, 2, 4, 8, 16, 32, 64]
C_ID, C_CAUS, C_LEV = 0, 128, 256
C_TRI = C_LEV + 128 * (len(LEVELS) + 1)
C_ONE, C_IOTA, C_IOTA8, C_INVF, C_COS, C_SIN, C_EPS = (C_TRI + x for x in (128, 256, 288, 296, 328, 392, 456))
NCONST = C_EPS + 1


def shape_constants():
    c = np.zeros((P, NCONST), np.float32)
    i = np.arange(P)
    row, col = i[:, None], i[None, :]
    c[:, C_ID:C_ID + P] = row == col
    c[:, C_CAUS:C_CAUS + P] = np.where(col <= row, 0.0, NEG)
    c[:, C_LEV:C_LEV + P] = row == col
    for n, b in enumerate(LEVELS):
        pair = (row // (2 * b) == col // (2 * b)) & (row % (2 * b) < b) & (col % (2 * b) >= b)
        c[:, C_LEV + P * (n + 1):C_LEV + P * (n + 2)] = pair
    c[:, C_TRI:C_TRI + P] = row < col
    c[:, C_ONE:C_ONE + P] = 1.0
    c[:, C_IOTA:C_IOTA + CAP] = np.arange(CAP)
    c[:, C_IOTA8:C_IOTA8 + 8] = np.arange(8)
    half = 32
    inv = (10000.0 ** (-np.arange(half, dtype=np.float64) / half)).astype(np.float32)
    c[:, C_INVF:C_INVF + half] = inv
    for t in range(NT):
        ang = ((i + t * P).astype(np.float32)[:, None] * inv).astype(np.float64)
        c[:, C_COS + half * t:C_COS + half * (t + 1)] = np.cos(ang)
        c[:, C_SIN + half * t:C_SIN + half * (t + 1)] = np.sin(ang)
    c[:, C_EPS] = EPS
    return c


def units_1():
    u = [(f"hf{i}", "w_in", 1024 + 512 * i, 512, 8) for i in range(2)]
    u += [(f"hq{i}", "w_in", 512 * i, 512, 8) for i in range(2)]
    u += [(f"hv{i}", "w_in", 2048 + 512 * i, 512, 8) for i in range(2)]
    u += [("cl", "w_in", 4096, 512, 8), ("ch", "w_in", 4608, 192, 8)]
    u += [(f"hg{i}", "w_in", 3072 + 512 * i, 512, 8) for i in range(2)]
    u += [(f"ga{i}", "w_in", 4800 + 512 * i, 512, 8) for i in range(2)]
    u += [(f"gb{i}", "w_in", 5824 + 512 * i, 512, 8) for i in range(2)]
    u += [("uq0", "mla_w_uq", 0, 768, 3), ("uq1", "mla_w_uq", 768, 768, 3), ("ukv", "mla_w_ukv", 0, 2048, 2)]
    u += [(f"wa{i}", "w_branch_hgrn", 512 * i, 512, 8) for i in range(2)]
    u += [(f"wb{i}", "w_branch_mla", 512 * i, 512, 8) for i in range(2)]
    u += [(f"wo{i}", "w_out", 512 * i, 512, 8) for i in range(2)]
    u += [("rt", "router", 0, 72, 8)]
    return u


def units_2():
    u = [("iq", 4096), ("ikw", 4608), ("dq", 2048), ("dv", 3072), ("dk", 2560), ("mv", 1024), ("mq", 0),
         ("dg", 3584), ("mk", 512), ("mg", 1536)]
    u = [(n, "w_in_2", c, 72 if n == "ikw" else 512, 8) for n, c in u]
    u += [("xk", "w_mem_kv_2", 0, 512, 8), ("xv", "w_mem_kv_2", 512, 512, 8)]
    u += [("xq", "w_in_2", 4680, 512, 8), ("xg", "w_in_2", 5192, 512, 8)]
    u += [(f"gl{i}", "w_in_2", 5704 + 512 * i, 512, 8) for i in range(6)]
    u += [("um", "w_up_moba_2", 0, 1024, 4), ("ud", "w_up_dsa_2", 0, 1024, 4), ("ux", "w_up_cross_2", 0, 1024, 4)]
    u += [(f"w2{i}", "w_out_2", 512 * i, 512, 8) for i in range(2)]
    return u


UNITS_1, UNITS_2 = units_1(), units_2()

CAUSAL = [(0, 0, 8, 1), (1, 0, 4, 2), (1, 4, 4, 2)]
CROSS = [(0, 0, 4, 2), (1, 0, 4, 2)]
CHUNKS = [("mla", c) for c in CAUSAL] + [("dsa", c) for c in CAUSAL] + [("moba", c) for c in CAUSAL] + \
         [("cross", c) for c in CROSS]


def slots(kind, nh):
    return list(range(nh)) if kind == "cross" else [*range(0, nh, 2), *range(1, nh, 2)]


def index_at(i, nk):
    return i % 2, (i // 2) * nk


def plan():
    p = []

    def proj(*names):
        p.extend(("proj", n, "P") for n in names)

    def soft(g):
        p.extend([("scores", g, "A"), ("soft", g, "")])

    def rest(g):
        p.extend([("normal", g, ""), ("probsT", g, "B"), ("pv", g, "B")])

    p.append(("norm", "x", "AB"))
    proj("hf0", "hf1", "hq0", "hq1")
    p.append(("level", 0, "AB"))
    fill = [["hv0"], ["hv1"], ["cl"], ["ch"], ["hg0", "hg1"], ["ga0"], ["ga1"], ["gb0"]]
    for n in range(1, len(LEVELS) + 2):
        proj(*fill[n - 1])
        p.append(("level", n, "AB" if n <= len(LEVELS) else "A"))
    p.append(("cnorm", 0, "AB"))
    p.append(("hg_out", 0, "AB"))
    proj("gb1")
    proj("uq0n", "uq0p", "uq1n", "uq1p")
    p.append(("hg_outT", 0, "AB"))
    p.append(("qkpT", 0, "AB"))
    proj("kn0", "kn1")
    soft(0)
    proj("vm0", "vm1")
    soft(1)
    rest(0)
    proj("wa0")
    soft(2)
    rest(1)
    proj("wa1")
    rest(2)
    proj("wb0", "wb1")
    p.append(("norm", "mem", "AB"))
    proj("wo0", "wo1")
    p.append(("norm", "ffn", "AB"))
    proj("rt")
    p.append(("rank", 0, "A"))
    p.append(("moe", 0, ""))
    p.append(("norm", "mid", "AB"))
    proj("iq", "ikw")
    p.append(("ropeT", "iq", "AB"))
    p.append(("ropeT", "ik", "AB"))
    proj("dq")
    p.extend([("index", 0, "A"), ("index", 1, "B")])
    proj("dv")
    p.append(("ropeT", "dq", "AB"))
    proj("dk")
    p.extend([("index", 2, "A"), ("index", 3, "B")])
    proj("mv")
    p.append(("ropeT", "dk", "AB"))
    proj("mq")
    p.extend([("index", 4, "A"), ("index", 5, "B")])
    proj("dg")
    p.append(("ropeT", "mq", "AB"))
    proj("mk", "mg")
    p.append(("ropeT", "mk", "AB"))
    proj("xk")
    soft(6)
    p.append(("topk", 0, ""))
    soft(7)
    rest(6)
    proj("xv")
    soft(8)
    rest(7)
    proj("xq")
    soft(3)
    rest(8)
    proj("xg")
    soft(4)
    rest(3)
    proj("gl0")
    soft(5)
    rest(4)
    proj("gl1")
    soft(9)
    rest(5)
    proj("gl2")
    soft(10)
    rest(9)
    proj("gl3")
    rest(10)
    proj("gl4", "gl5")
    proj("um0", "um1", "ud0", "ud1", "ux0", "ux1", "w20", "w21")
    p.append(("final", 0, ""))
    return p


PLAN = plan()
USE, FULL_AT = {}, {}


def count_uses():
    n = dict.fromkeys(("P0", "P1", "A", "B"), 0)
    turn = 0
    for name, arg, regions in PLAN:
        use = {}
        for r in regions:
            if r == "P":
                r, turn = f"P{turn}", 1 - turn
            n[r] += 1
            use[r] = n[r]
        USE[name, arg] = use


count_uses()

SEQ = {g: n for n, g in enumerate(arg for name, arg, _ in PLAN if name == "scores")}
AT = {n: g for g, n in SEQ.items()}

STEP_UNIT = {f"uq{i}{c}": f"uq{i}" for i in range(2) for c in "np"}
STEP_UNIT |= {n: "ukv" for n in ("kn0", "kn1", "vm0", "vm1")}
STEP_UNIT |= {f"u{c}{i}": f"u{c}" for c in "mdx" for i in range(2)}
LAST = {"uq0": "uq0p", "uq1": "uq1p", "ukv": "vm1", "um": "um1", "ud": "ud1", "ux": "ux1"}

MOE_UNITS = [(0, "w1"), (0, "w3"), (1, "w1"), (1, "w3"), (0, "w2"), (2, "w1"), (2, "w3"), (1, "w2"),
             (3, "w1"), (3, "w3"), (2, "w2"), (3, "w2")]
MOE_AT = {x: n for n, x in enumerate(MOE_UNITS)}
NU = len(MOE_UNITS)


def build(nc, ins, out):
    with ExitStack() as ctx:
        def sb(name, shape, dt=F32):
            return ctx.enter_context(nc.sbuf_tensor(name, shape, dt))

        def sem(name):
            return ctx.enter_context(nc.semaphore(name))

        ring = sb("ring", [P, SLOTS, SLOT])
        X = sb("X", [P, NT, D])
        consts = sb("consts_sb", [P, NCONST])
        arena = sb("arena", [P, 14 * 2048])
        small = sb("small", [P, 512])
        vec = sb("vec", [P, 128])
        rbias = sb("rbias", [P, 72])
        rope1 = sb("rope1", [P, 4, 64])
        idx8 = sb("idx8", [P, 8], U32)
        ints = sb("ints", [P, 4], I32)

        def area(a, *shape, off=0):
            n = int(np.prod(shape))
            ap = arena[:, a * 2048 + off:a * 2048 + off + n]
            if len(shape) == 1:
                return ap
            names = "abcd"[:len(shape)]
            kw = {names[i]: shape[i] for i in range(len(shape))}
            return ap.rearrange(f"p ({' '.join(names)}) -> p {' '.join(names)}", **kw)

        hT = area(12, KC, S)
        pre, suf, hq, hk = area(0, HH, S), area(1, HH, S), area(2, HH, S), area(3, HH, S)
        lq, lk, hv = area(4, HH, S), area(5, HH, S), area(6, NT, D)
        hattn = area(7, 3, HH, P)
        GA, GB, GH = area(9, KC, S), area(10, KC, S), area(11, NT, D)
        C = area(13, NT, 704)
        hgo, hgsq, oaT = area(4, NT, D), area(5, NT, D), area(2, KC, S)
        cT = sb("cT", [P, 5, S])
        kpe2 = sb("kpe2", [P, NT, P])
        kpeT = sb("kpeT", [P, S])
        qn, kn, vm = area(0, HH, S), area(1, HH, S), area(3, NT, D)
        qpe, qpeT = area(5, NT, 512), area(5, 4, S, off=1024)
        soft_1, prT_1 = area(6, 2, 1024), area(11, 2, 8, P)
        obT, Y = area(4, KC, S), area(7, KC, S)
        xn = area(0, NT, D)
        xnf = area(0, NT, D)
        selA = arena[:, 2 * 2048:2 * 2048 + (GROUPS + 1) * NT * SEL].rearrange(
            "p (g t c) -> p g t c", g=GROUPS + 1, t=NT)
        selT = area(5, GROUPS, S)[:, :, :]
        selW = arena[:, 7 * 2048:9 * 2048].rearrange("p (g t c) -> p g t c", g=GROUPS, t=NT)
        xgT, gate_s, hid = area(9, KC, SEL), area(9, FF, off=1024), area(9, FF, off=1536)
        hidT = area(10, EG, 4, P)
        ysb, selTs = area(11, D), area(11, S, off=1024)
        L = area(12, NT, 72)
        lrow = area(12, NT, 8, off=256)
        memT = area(1, KC, S)
        mem = area(13, NT, D)
        xm, xo = area(0, NT, D), area(5, NT, D)
        qkT = {"iq": area(2, 4, S), "dq": area(2, 4, S, off=1024), "dk": area(3, 4, S),
               "mq": area(3, 4, S, off=1024), "mk": area(4, 4, S)}
        ikT = area(4, S, off=1024)
        ikr = area(4, NT, P, off=1280)
        iw = area(4, NT, 8, off=1536)
        dv, mv = area(5, NT, 512), area(5, NT, 512, off=1024)
        soft_2, prT_2 = area(6, 2, 1024), area(7, 2, 8, P)
        xqT, xkT, xv = area(8, 4, S), area(8, 4, S, off=1024), area(9, NT, 512)
        ropeA, ropeB = area(9, NT, 512, off=1024), area(13, NT, 512)
        relu_s = area(13, 2, 512, off=1024)
        score = sb("score", [P, 384])
        dmask = sb("dmask", [P, 384])
        sg = {"mg": area(10, 4, S), "dg": area(10, 4, S, off=1024), "xg": area(11, 4, S)}
        utmp = area(11, 4, S, off=1024)
        gl = [area(0, KC, S), area(1, KC, S), area(2, KC, S)]
        wrow, wrow_f = area(4, D, off=1024), area(13, D, off=1024)

        ps = {"P0": ctx.enter_context(nc.psum_tensor("psP0", [P, 1024], F32)),
              "P1": ctx.enter_context(nc.psum_tensor("psP1", [P, 1024], F32)),
              "A": ctx.enter_context(nc.psum_tensor("psA", [P, 1024], F32)),
              "B": ctx.enter_context(nc.psum_tensor("psB", [P, 1024], F32))}

        ident = consts[:, C_ID:C_ID + P]
        caus = consts[:, C_CAUS:C_CAUS + P]
        eps = consts[:, C_EPS:C_EPS + 1]

        V_ATT, V_FFN, V_IN2, V_MEM, V_HGN, V_LB0, V_LB1, V_LB, V_OML, V_QN, V_KVN, V_BM = (
            0, 8, 16, 24, 32, 40, 48, 56, 64, 72, 75, 80)

        full = {r: sem(f"full_{r}") for r in ps}
        empty = {r: sem(f"empty_{r}") for r in ps}
        landed = [sem(f"landed_{i}") for i in range(SLOTS)]
        landed2 = [sem(f"landed2_{i}") for i in range(SLOTS)]
        x_in, consts_in, vec_in, mem_in = sem("x_in"), sem("consts_in"), sem("vec_in"), sem("mem_in")
        row_in = sem("row_in")
        dve_seq, act_seq = sem("dve_seq"), sem("act_seq")
        squares, roots = sem("squares"), sem("roots")
        normed = sem("normed")
        lb_diff, lb_sig = sem("lb_diff"), sem("lb_sig")
        angles, sines = sem("angles"), sem("sines")
        hg_sig, hg_ready = sem("hg_sig"), sem("hg_ready")
        o_sq, o_done = sem("o_sq"), sem("o_done")
        sm_max, sm_exp, probs = sem("sm_max"), sem("sm_exp"), sem("probs")
        roped = sem("roped")
        relus = sem("relus")
        rt_max, rt_exp, rt_mask = sem("rt_max"), sem("rt_exp"), sem("rt_mask")
        rt_max2, rt_exp2 = sem("rt_max2"), sem("rt_exp2")
        rounds_ready = sem("rounds_ready")
        sel_ready, selT_full, selT_empty = sem("sel_ready"), sem("selT_full"), sem("selT_empty")
        products, gathered, xg_ready = sem("products"), sem("gathered"), sem("xg_ready")
        silu_done, hid_done, hidT_full, hidT_ready = sem("silu_done"), sem("hid_done"), sem("hidT_full"), sem("hidT_ready")
        y_half, y_copied, scattered, added = sem("y_half"), sem("y_copied"), sem("scattered"), sem("added")
        selTs_ready = sem("selTs_ready")
        o_summed, index_added, sel_step = sem("o_summed"), sem("index_added"), sem("sel_step")
        stream_scaled = sem("stream_scaled")
        ONE_UP = {"pe": (gathered, hidT_full, scattered), "act": (y_copied, selT_empty),
                  "dve": (added, hid_done, hidT_ready, sel_step)}

        def one_up(e, name):
            for s in ONE_UP[name]:
                e.sem_inc(s, 1)
        stored = sem("stored")

        block = ctx.enter_context(nc.Block())

        def wait_full(e, key, region=None):
            for r, n in USE[key].items():
                if region in (None, r):
                    e.wait_ge(full[r], n)

        def wait_empty(e, key, region=None):
            for r, n in USE[key].items():
                if region in (None, r):
                    e.wait_ge(empty[r], n)

        def region_of(key):
            return list(USE[key])[0]

        def may_fill(e, key, region=None):
            for r, n in USE[key].items():
                if region in (None, r) and n > 1:
                    e.wait_ge(empty[r], n - 1)

        def bc(ap, shape, axis):
            return ap.unsqueeze(axis).broadcast_to(shape)

        unit_at = {}
        for lands, units in ((landed, UNITS_1), (landed2, UNITS_2)):
            for n, u in enumerate(units):
                unit_at[u[0]] = (n % SLOTS, lands[n % SLOTS], 16 * (n // SLOTS + 1) * (2 if u[0] == "rt" else 1), u)
        n_rt = len(UNITS_1) - 1
        unit_at["rt"] = (n_rt % SLOTS, landed[n_rt % SLOTS], 16 * (n_rt // SLOTS) + 32, UNITS_1[n_rt])
        MOE_LAND = [16 * len([n for n in range(len(UNITS_1)) if n % SLOTS == s]) + (16 if s == n_rt % SLOTS else 0)
                    for s in range(SLOTS)]
        assert len(UNITS_1) % SLOTS == 0 and NU % SLOTS == 0

        def unit_ap(name):
            slot, _, _, (_, _, _, cols, kc) = unit_at[name]
            return ring[:, slot, 0:kc * cols].rearrange("p (k n) -> p k n", k=kc)

        def wait_unit(e, name):
            e.wait_ge(unit_at[name][1], unit_at[name][2])

        def chunk_stats(g):
            base = 64 + 24 * (SEQ[g] % 2)
            return [small[:, base + 8 * i:base + 8 * i + CHUNKS[g][1][2]] for i in range(3)]

        def moe_tensor(pe):
            zG, zU = ps["P0"][:, 0:512], ps["P0"][:, 512:1024]
            zY, zA, zB = ps["P1"], ps["A"], ps["B"]

            def gather(g):
                for k in range(KC):
                    for t in range(NT):
                        mm = pe.matmul(zA[:, k * P:(k + 1) * P], xnf[:, t, k::KC],
                                       selA[:, g, t, :] if isinstance(g, int) else
                                       selA[:, bass.ds(g, 1), t, :].rearrange("p g c -> p (g c)"),
                                       start=(t == 0), stop=(t == NT - 1))
                mm.then_inc(gathered, 1)

            wait_empty(pe, ("rank", 0))
            wait_empty(pe, ("norm", "ffn"))
            wait_empty(pe, ("proj", "wo1"))
            wait_empty(pe, ("proj", "rt"))
            pe.wait_ge(rounds_ready, 1)
            rounds = pe.value_load(ints[0:1, 2:3], min_val=0, max_val=S // CAP - 1) + 1
            one_up(pe, "pe")
            with pe.Fori(0, rounds) as r:
                pe.wait_ge(added, r * (4 * GROUPS) + 1)
                pe.wait_ge(sel_ready, r + 1)
                for f in range(8):
                    pe.wait_ge(selT_empty, r * 8 + (f - 1 if f else 0) + 1)
                    z = zB[:, (f % 2) * 512:(f % 2 + 1) * 512]
                    for i in range(4):
                        mm = pe.transpose(z[:, i * P:(i + 1) * P], selW[:, 2 * f + i // 2, i % 2, :], ident)
                    mm.then_inc(selT_full, 1)
                pe.wait_ge(selT_empty, r * 8 + 8 + 1)
                gather(0)
                with pe.Fori(0, GROUPS) as g:
                    it = pe.snap(r * GROUPS + g)

                    for j in range(EG):
                        for which, z in (("w1", zG), ("w3", zU)):
                            n = MOE_AT[j, which]
                            w = ring[:, n % SLOTS, :].rearrange("p (k n) -> p k n", k=KC)
                            if j == 0 and which == "w1":
                                pe.wait_ge(xg_ready, it + r + 1)
                            if which == "w1":
                                pe.wait_ge(hid_done, it * EG + j + 1)
                            pe.wait_ge(landed[n % SLOTS], it * (16 * NU // SLOTS) + (MOE_LAND[n % SLOTS] + 16 * (n // SLOTS + 1)))
                            for k in range(KC):
                                mm = pe.matmul(z[0:CAP, :], xgT[:, k, j * CAP:(j + 1) * CAP], w[:, k, :],
                                               start=(k == 0), stop=(k == KC - 1))
                            mm.then_inc(products, 1)
                        if j == EG - 1:
                            pe.wait_ge(added, it * 4 + 1)
                            gather(g + 1)
                        if j:
                            down(pe, it, j - 1, zY)
                        pe.wait_ge(hidT_ready, it * EG + j + 1)
                        pe.wait_ge(hid_done, it * EG + (j + 1) + 1)
                        for c in range(4):
                            mm = pe.transpose(zB[:, c * P:(c + 1) * P], hid[:, c::4], ident)
                        mm.then_inc(hidT_full, 1)
                    down(pe, it, EG - 1, zY)
                    dsts = [(0, 0, zB[:, 512:1024]), (1, 0, zA[:, 0:512]), (0, 1, zA[:, 512:1024]), (1, 1, zB[:, 512:1024])]
                    pe.wait_ge(selTs_ready, it + 1)
                    pe.wait_ge(xg_ready, it + r + 2)
                    for n, (t, half, z) in enumerate(dsts):
                        if n % 2 == 0:
                            pe.wait_ge(y_copied, it * 2 + (half + 1) + 1)
                        if n == 3:
                            pe.wait_ge(added, it * 4 + 1 + 1)
                        pe.matmul(z, selTs[:, t * P:(t + 1) * P], ysb[:, half * 512:(half + 1) * 512],
                                  start=True, stop=True).then_inc(scattered, 1)

        def down(pe, it, j, zY):
            n = MOE_AT[j, "w2"]
            w = ring[:, n % SLOTS, :].rearrange("p (k n) -> p k n", k=4)
            pe.wait_ge(landed[n % SLOTS], it * (16 * NU // SLOTS) + (MOE_LAND[n % SLOTS] + 16 * (n // SLOTS + 1)))
            pe.wait_ge(hidT_ready, it * EG + (j + 1) + 1)
            if j == 0:
                pe.wait_ge(y_copied, it * 2 + 1)
            for half in range(2):
                for c in range(4):
                    mm = pe.matmul(zY[:, half * 512:(half + 1) * 512], hidT[:, j, c, :], w[:, c, half * 512:(half + 1) * 512],
                                   start=(j == 0 and c == 0), stop=(j == EG - 1 and c == 3))
                if half:
                    mm.then_inc(products, 1)
                elif j == EG - 1:
                    mm.then_inc(y_half, 1)

        def route(dve, link, tt):
            iota8 = consts[:, C_IOTA8:C_IOTA8 + 8]
            wait_empty(dve, ("proj", "rt"))
            oneG, one0, one1 = (area(12, NT, 8, off=o) for o in (320, 336, 352))
            esel = area(12, NT, 8, off=368)
            m8 = area(12, NT, 8, off=384)
            m8b = area(12, NT, 8, off=400)
            fidx = area(12, NT, off=416)
            prod = area(12, 64, off=1024)
            M, W = area(12, NT, 64, off=512), area(12, NT, 64, off=640)
            pos = area(12, NT, 64, off=768)

            def first_of(row, top, t):
                link(dve.max(top, row))
                link(dve.max_index(idx8[:, :], top, row))
                link(dve.tensor_copy(fidx[:, t:t + 1], idx8[:, 0:1]))

            for t in range(NT):
                first_of(L[:, t, 0:8], m8[:, t, :], t)
                link(dve.tensor_scalar(oneG[:, t, :], iota8, fidx[:, t:t + 1], None, ALU.is_equal))
            dve.tensor_scalar(small[:, 208:210].unsqueeze(2), m8[:, :, 0:1], -1.0, None, ALU.mult).then_inc(rt_max, 1)
            for t in range(NT):
                p3 = prod.rearrange("p (e g) -> p e g", g=8)
                link(tt(p3, L[:, t, 8:72].rearrange("p (g e) -> p e g", g=8), bc(oneG[:, t, :], [P, 8, 8], 1), ALU.mult))
                link(dve.tensor_reduce(esel[:, t, :], p3, AX.X, ALU.add))
                first_of(esel[:, t, :], m8[:, t, :], t)
                link(dve.tensor_scalar(one0[:, t, :], iota8, fidx[:, t:t + 1], None, ALU.is_equal))
                link(dve.scalar_tensor_tensor(out=esel[:, t, :], in0=one0[:, t, :], scalar=USED, in1=esel[:, t, :],
                                              op0=ALU.mult, op1=ALU.add))
                first_of(esel[:, t, :], m8b[:, t, :], t)
                link(dve.tensor_scalar(one1[:, t, :], iota8, fidx[:, t:t + 1], None, ALU.is_equal))
            tt(small[:, 212:214].unsqueeze(2), m8b[:, :, 0:1], m8[:, :, 0:1], ALU.subtract).then_inc(rt_max2, 1)
            link(tt(esel[:, :, :], one0[:, :, :], one1[:, :, :], ALU.add))
            for t in range(NT):
                i = tt(M[:, t, :].rearrange("p (g e) -> p g e", g=8), bc(oneG[:, t, :], [P, 8, 8], 2),
                       bc(esel[:, t, :], [P, 8, 8], 1), ALU.mult)
            i.then_inc(rt_mask, 1)
            dve.wait_ge(rt_exp, 1)
            dve.wait_ge(rt_exp2, 1)
            gw, e2 = small[:, 210:212], small[:, 214:216]
            link(dve.tensor_scalar(small[:, 216:218], e2, 1.0, None, ALU.add))
            link(tt(small[:, 216:218], small[:, 216:218], gw, ALU.mult))
            link(dve.reciprocal(small[:, 216:218], small[:, 216:218]))
            link(tt(small[:, 218:220], small[:, 216:218], e2, ALU.mult))
            for t in range(NT):
                link(dve.tensor_scalar(one0[:, t, :], one0[:, t, :], small[:, 216 + t:217 + t], None, ALU.mult))
                link(dve.scalar_tensor_tensor(out=one1[:, t, :], in0=one1[:, t, :], scalar=small[:, 218 + t:219 + t],
                                              in1=one0[:, t, :], op0=ALU.mult, op1=ALU.add))
                link(tt(W[:, t, :].rearrange("p (g e) -> p g e", g=8), bc(oneG[:, t, :], [P, 8, 8], 2),
                        bc(one1[:, t, :], [P, 8, 8], 1), ALU.mult))
            wait_full(dve, ("rank", 0))
            z = ps["A"]
            p2 = pos.rearrange("p t e -> p (t e)")
            link(dve.tensor_scalar(p2, z[:, 0:128], 1.0, None, ALU.add))
            link(tt(p2, p2, M.rearrange("p t e -> p (t e)"), ALU.mult))
            link(dve.tensor_scalar(p2, p2, -1.0, None, ALU.add))
            link(dve.tensor_reduce(small[:, 220:221], z[:, 128:192], AX.X, ALU.max))
            link(dve.tensor_scalar(small[:, 220:221], small[:, 220:221], -float(CAP), None, ALU.add))
            link(dve.tensor_scalar(small[:, 224:232], iota8, float(CAP), small[:, 220:221], ALU.mult, ALU.is_lt))
            link(dve.tensor_reduce(small[:, 221:222], small[:, 224:232], AX.X, ALU.add))
            dve.tensor_copy(ints[:, 2:3], small[:, 221:222]).then_inc(rounds_ready, 1)
            dve.wait_ge(rounds_ready, 1)
            link(dve.memset(hidT[:, :, :, :], 0.0))
            link(dve.memset(hid[:, :], 0.0))
            dve.memset(selA[:, GROUPS, :, :], 0.0).then_inc(empty["A"], 1)

        def experts(dve, link, tt):
            M, W = area(12, NT, 64, off=512), area(12, NT, 64, off=640)
            pos = area(12, NT, 64, off=768)
            iota = consts[:, C_IOTA:C_IOTA + CAP]
            rounds = dve.value_load(ints[0:1, 2:3], min_val=0, max_val=S // CAP - 1) + 1
            one_up(dve, "dve")
            with dve.Fori(0, rounds) as r:
                dve.wait_ge(gathered, r * (GROUPS + 1) + 1)
                dve.wait_ge(sel_step, r * 2 + 1)
                for t in range(NT):
                    a = selA[:, 0:GROUPS, t, :].rearrange("p g (j c) -> p g j c", c=CAP)
                    p4 = pos[:, t, :].rearrange("p (g j) -> p g j", j=EG).unsqueeze(3).broadcast_to([P, GROUPS, EG, CAP])
                    i4 = iota.unsqueeze(1).unsqueeze(1).broadcast_to([P, GROUPS, EG, CAP])
                    x = tt(a, i4, p4, ALU.is_equal)
                x.then_inc(sel_step, 1)
                dve.wait_ge(sel_step, r * 2 + 1 + 1)
                for t in range(NT):
                    a = selA[:, 0:GROUPS, t, :].rearrange("p g (j c) -> p g j c", c=CAP)
                    b = selW[:, :, t, :].rearrange("p g (j c) -> p g j c", c=CAP)
                    w4 = W[:, t, :].rearrange("p (g j) -> p g j", j=EG).unsqueeze(3).broadcast_to([P, GROUPS, EG, CAP])
                    x = tt(b, a, w4, ALU.mult)
                x.then_inc(sel_ready, 1)
                dve.tensor_scalar(pos, pos, -float(CAP), None, ALU.add).then_inc(sel_step, 1)
                dve.wait_ge(selT_empty, r * 8 + 8 + 1)
                dve.wait_ge(gathered, r * (GROUPS + 1) + 1 + 1)
                gathered_rows(dve, tt)
                with dve.Fori(0, GROUPS) as g:
                    it = dve.snap(r * GROUPS + g)
                    dve.wait_ge(scattered, it * 4 + 1)
                    dve.tensor_scalar(selTs, selT[:, bass.ds(g, 1), :].rearrange("p g n -> p (g n)"), 1.0, None,
                                      ALU.mult).then_inc(selTs_ready, 1)
                    for j in range(EG):
                        dve.wait_ge(hidT_full, it * EG + j + 1)
                        dve.wait_ge(silu_done, it * EG + (j + 1))
                        dve.wait_ge(products, it * NU + (MOE_AT[j, "w3"] + 1))
                        tt(hid[0:CAP, :], gate_s[0:CAP, :], ps["P0"][0:CAP, 512:1024], ALU.mult).then_inc(hid_done, 1)
                        if j == EG - 1:
                            dve.wait_ge(gathered, it + r + 2 + 1)
                            gathered_rows(dve, tt)
                        dve.wait_ge(hidT_full, it * EG + (j + 1) + 1)
                        dve.tensor_copy(hidT[:, j, :, j * CAP:(j + 1) * CAP],
                                        ps["B"][:, 0:512].rearrange("p (c n) -> p c n", c=4)[:, :, 0:CAP]).then_inc(hidT_ready, 1)
                    for n, (t, half, z) in enumerate([(0, 0, ps["B"][:, 512:1024]), (1, 0, ps["A"][:, 0:512]),
                                                      (0, 1, ps["A"][:, 512:1024]), (1, 1, ps["B"][:, 512:1024])]):
                        dve.wait_ge(scattered, it * 4 + (n + 1) + 1)
                        dst = X[:, t, half * 512:(half + 1) * 512]
                        tt(dst, dst, z, ALU.add).then_inc(added, 1)
            return rounds

        def gathered_rows(dve, tt):
            tt(xgT[:, :, :], ps["A"][:, :].rearrange("p (k n) -> p k n", k=KC),
               bc(vec[:, V_FFN:V_FFN + KC], [P, KC, SEL], 2), ALU.mult).then_inc(xg_ready, 1)

        @block.sync
        def _(sp):
            sp.dma_start(X[:, :, :], ins["x"][0].rearrange("(t p) d -> p t d", p=P)).then_inc(x_in, 16)

            def load(units, n):
                name, tensor, c0, cols, kc = units[n]
                if n >= SLOTS:
                    prev = units[n - SLOTS][0]
                    key = ("proj", LAST.get(prev, prev))
                    r = region_of(key)
                    sp.wait_ge(full[r], USE[key][r])
                slot, land, _, _ = unit_at[name]
                dst = ring[:, slot, 0:kc * cols].rearrange("p (k n) -> p k n", k=kc)
                if name == "rt":
                    sp.dma_start(dst[:, :, 0:8], ins["router_group_w"][0].rearrange("(p k) n -> p k n", k=KC)).then_inc(land, 16)
                    sp.dma_start(dst[:, :, 8:72], ins["router_expert_w"][0].rearrange("(p k) n -> p k n", k=KC)).then_inc(land, 16)
                    return
                src = ins[tensor][0][:, c0:c0 + cols].rearrange("(k p) n -> p k n", p=P)
                sp.dma_start(dst, src).then_inc(land, 16)

            for n in range(len(UNITS_1)):
                if UNITS_1[n][0] == "wb0":
                    wait_full(sp, ("cnorm", 0))
                    sp.wait_ge(roped, 1)
                    sp.dma_start(mem[:, :, :], ins["mem_2"][0].rearrange("(t p) d -> p t d", p=P)).then_inc(mem_in, 16)
                load(UNITS_1, n)
            wait_full(sp, ("proj", "wb1"))
            sp.dma_start(wrow, ins["final_norm_w"].unsqueeze(0).broadcast_to([P, D])).then_inc(row_in, 16)

            ew = {"w1": ins["expert_w1"][0].rearrange("e (p k) n -> e p (k n)", k=KC),
                  "w3": ins["expert_w3"][0].rearrange("e (p k) n -> e p (k n)", k=KC),
                  "w2": ins["expert_w2"][0].rearrange("e (p k) n -> e p (k n)", k=4)}

            def group_loads(r, g, peeled):
                for n, (j, which) in enumerate(MOE_UNITS):
                    if peeled and n < SLOTS:
                        prev = UNITS_1[len(UNITS_1) - SLOTS + n][0]
                        key = ("proj", LAST.get(prev, prev))
                        reg = region_of(key)
                        sp.wait_ge(full[reg], USE[key][reg])
                    else:
                        sp.wait_ge(products, r * (GROUPS * NU) + g * NU + (n - SLOTS + 1))
                    src = ew[which][j] if peeled else ew[which][bass.ds(g * EG + j, 1)].rearrange("e p n -> p (e n)")
                    sp.dma_start(ring[:, n % SLOTS, :], src).then_inc(landed[n % SLOTS], 16)

            group_loads(0, 0, True)
            with sp.Fori(1, GROUPS) as g:
                group_loads(0, g, False)
            sp.wait_ge(rounds_ready, 1)
            rounds = sp.value_load(ints[0:1, 2:3], min_val=0, max_val=S // CAP - 1) + 1
            with sp.If(rounds > 1):
                with sp.Fori(1, rounds) as r:
                    with sp.Fori(0, GROUPS) as g:
                        group_loads(r, g, False)
            for n in range(len(UNITS_2)):
                if n < SLOTS:
                    sp.wait_ge(products, rounds * (GROUPS * NU) - (SLOTS - 1 - n))
                if UNITS_2[n][0] == "um":
                    sp.wait_ge(index_added, 6)
                    sp.dma_start(wrow_f, ins["g_final_2"].unsqueeze(0).broadcast_to([P, D])).then_inc(row_in, 16)
                load(UNITS_2, n)
            sp.wait_ge(normed, 6)
            sp.dma_start(out[0].rearrange("(t p) d -> p t d", p=P), xo[:, :, :]).then_inc(stored, 16)
            sp.wait_ge(stored, 16)

        @block.tensor
        def _(pe):
            def transposes(key, src_of, region, n, done=True):
                may_fill(pe, key, region)
                for i in range(n):
                    mm = pe.transpose(ps[region][:, i * P:(i + 1) * P], src_of(i), ident)
                mm.then_inc(full[region], 1)

            def proj(key, name, lhs_of, rhs_of, kc, outs):
                may_fill(pe, key)
                r = region_of(key)
                for o in range(len(outs(ps[r]))):
                    dst = outs(ps[r])[o]
                    for k in range(kc):
                        mm = pe.matmul(dst, lhs_of(o, k), rhs_of(o, k), start=(k == 0), stop=(k == kc - 1))
                mm.then_inc(full[r], 1)

            def rows_out(cols):
                return lambda z: [z[:, t * 512:t * 512 + cols] for t in range(NT)]

            def feats_out(z):
                return [z[:, c * S:(c + 1) * S] for c in range(4)]

            def feature_major(key, name, src, kc=8, c0=0, stride=P):
                w = unit_ap(STEP_UNIT.get(name, name))
                proj(key, name, lambda o, k: w[:, k, c0 + o * stride:c0 + o * stride + P],
                     lambda o, k: src[:, k, :], kc, feats_out)

            def token_major(key, name, src, kc=8, w=None, cols=512):
                w = unit_ap(name) if w is None else w
                proj(key, name, lambda o, k: src[:, k, o * P:(o + 1) * P],
                     lambda o, k: w[:, k], kc, rows_out(cols))

            rope_n = {"iq": 1, "ik": 1, "dq": 2, "dk": 3, "mq": 4, "mk": 5}

            for name, arg, _ in PLAN:
                key = (name, arg)
                if name == "norm":
                    if arg == "x":
                        pe.wait_ge(consts_in, 16)
                    pe.wait_ge(normed, {"x": 1, "mem": 3, "ffn": 4, "mid": 5}[arg])
                    src = {"x": xn, "ffn": xnf, "mem": mem, "mid": xm}[arg]
                    for t, r in enumerate("AB"):
                        pick = (lambda i, t=t: src[:, t, i::KC]) if arg == "ffn" else \
                               (lambda i, t=t: src[:, t, i * P:(i + 1) * P])
                        transposes(key, pick, r, KC)
                elif name == "proj":
                    unit = STEP_UNIT.get(arg, arg)
                    wait_unit(pe, unit)
                    if arg == "hf0":
                        wait_empty(pe, ("norm", "x"))
                    if arg in ("hf0", "hf1", "hq0", "hq1", "ga0", "ga1", "gb0", "gb1"):
                        feature_major(key, arg, hT)
                    elif arg in ("hv0", "hv1", "hg0", "hg1", "cl"):
                        token_major(key, arg, hT)
                    elif arg == "ch":
                        token_major(key, arg, hT, cols=192)
                    elif arg in ("uq0n", "uq1n"):
                        if arg == "uq0n":
                            wait_empty(pe, ("cnorm", 0))
                        feature_major(key, arg, cT, kc=3, stride=192)
                    elif arg in ("uq0p", "uq1p"):
                        w = ring[:, unit_at[unit][0], 0:3 * 768].rearrange("p (k h c) -> p k h c", k=3, h=4)[:, :, :, P:192]
                        token_major(key, arg, cT, kc=3, w=w, cols=256)
                    elif arg in ("kn0", "kn1"):
                        feature_major(key, arg, cT[:, 3:5, :], kc=2, c0=1024 * int(arg[2]), stride=256)
                    elif arg in ("vm0", "vm1"):
                        i = int(arg[2])
                        w = ring[:, unit_at[unit][0], :].rearrange("p (k h c) -> p k h c", k=2, h=8)[:, :, 4 * i:4 * i + 4, P:256]
                        token_major(key, arg, cT[:, 3:5, :], kc=2, w=w)
                    elif arg in ("wa0", "wa1"):
                        if arg == "wa0":
                            wait_empty(pe, ("hg_outT", 0))
                        feature_major(key, arg, oaT)
                    elif arg in ("wb0", "wb1"):
                        if arg == "wb0":
                            wait_empty(pe, ("pv", 2))
                        feature_major(key, arg, obT)
                    elif arg in ("wo0", "wo1"):
                        if arg == "wo0":
                            wait_empty(pe, ("proj", "wb0"))
                            wait_empty(pe, ("proj", "wb1"))
                        token_major(key, arg, Y)
                    elif arg == "rt":
                        wait_empty(pe, ("norm", "ffn"))
                        token_major(key, arg, hT, cols=72)
                    elif arg in ("iq", "dq", "dk", "dv", "mq", "mk", "mv"):
                        if arg == "iq":
                            wait_empty(pe, ("norm", "mid"))
                        token_major(key, arg, hT)
                    elif arg == "ikw":
                        token_major(key, arg, hT, cols=72)
                    elif arg in ("xq", "mg", "dg", "xg") or arg[:2] == "gl":
                        feature_major(key, arg, hT)
                    elif arg == "xk":
                        wait_empty(pe, ("norm", "mem"))
                        feature_major(key, arg, memT)
                    elif arg == "xv":
                        token_major(key, arg, memT)
                    elif arg[0] == "u":
                        kind = {"m": "mg", "d": "dg", "x": "xg"}[arg[1]]
                        last = {"m": 8, "d": 5, "x": 10}[arg[1]]
                        if arg[2] == "0":
                            wait_empty(pe, ("pv", last))
                        feature_major(key, arg, sg[kind], kc=4, c0=512 * int(arg[2]))
                    elif arg in ("w20", "w21"):
                        if arg == "w20":
                            wait_empty(pe, ("proj", "ux0"))
                            wait_empty(pe, ("proj", "ux1"))
                        token_major(key, arg, gl[0])
                elif name == "level":
                    n = arg
                    if n:
                        pe.wait_ge(hg_ready, n + 1)
                    else:
                        pe.wait_ge(hg_ready, 1)
                    q, k = (lq, lk) if n else (hq, hk)
                    if n <= len(LEVELS):
                        for t, r in enumerate("AB"):
                            may_fill(pe, key, r)
                            for h in range(HH):
                                mm = pe.matmul(ps[r][:, h * P:(h + 1) * P], k[:, h, t * P:(t + 1) * P],
                                               q[:, h, t * P:(t + 1) * P], start=True, stop=True)
                            mm.then_inc(full[r], 1)
                    else:
                        may_fill(pe, key)
                        for h in range(HH):
                            mm = pe.matmul(ps["A"][:, h * P:(h + 1) * P], k[:, h, 0:P], q[:, h, P:S],
                                           start=True, stop=True)
                        mm.then_inc(full["A"], 1)
                elif name == "cnorm":
                    pe.wait_ge(normed, 2)
                    for t, r in enumerate("AB"):
                        transposes(key, lambda i, t=t: C[:, t, i * P:(i + 1) * P], r, 5)
                elif name == "hg_out":
                    wait_empty(pe, ("proj", "hv0"))
                    wait_empty(pe, ("proj", "hv1"))
                    wait_empty(pe, ("level", len(LEVELS)))
                    wait_empty(pe, ("level", len(LEVELS) + 1))
                    for t, r in enumerate("AB"):
                        may_fill(pe, key, r)
                        for h in range(HH):
                            dst = ps[r][:, h * P:(h + 1) * P]
                            if t:
                                pe.matmul(dst, hattn[:, 2, h, :], hv[:, 0, h * P:(h + 1) * P], start=True, stop=False)
                            mm = pe.matmul(dst, hattn[:, t, h, :], hv[:, t, h * P:(h + 1) * P], start=(t == 0), stop=True)
                        mm.then_inc(full[r], 1)
                elif name == "hg_outT":
                    pe.wait_ge(o_done, 1)
                    for t, r in enumerate("AB"):
                        transposes(key, lambda i, t=t: hgo[:, t, i * P:(i + 1) * P], r, 8)
                elif name == "qkpT":
                    pe.wait_ge(roped, 3)
                    for t, r in enumerate("AB"):
                        may_fill(pe, key, r)
                        for i in range(4):
                            pe.transpose(ps[r][:, i * P:(i + 1) * P], qpe[:, t, i * P:(i + 1) * P], ident)
                        pe.transpose(ps[r][:, 4 * P:5 * P], kpe2[:, t, :], ident).then_inc(full[r], 1)
                elif name == "ropeT":
                    pe.wait_ge(roped, {"iq": 4, "ik": 5, "dq": 6, "dk": 7, "mq": 8, "mk": 9}[arg])
                    for t, r in enumerate("AB"):
                        if arg == "ik":
                            transposes(key, lambda i, t=t: ikr[:, t, :], r, 1)
                        else:
                            transposes(key, lambda i, t=t: ropeA[:, t, i * P:(i + 1) * P], r, 4)
                elif name == "index":
                    if arg == 0:
                        wait_empty(pe, ("ropeT", "ik"))
                    may_fill(pe, key)
                    r = region_of(key)
                    t, h0, nh = (0, 4 * arg, 4) if arg < 2 else (1, 2 * (arg - 2), 2)
                    nk = P * (t + 1)
                    for i in range(nh):
                        h = h0 + i
                        lo = 64 * (h % 2)
                        bank, at = index_at(i, nk)
                        at += 512 * bank
                        mm = pe.matmul(ps[r][:, at:at + nk], qkT["iq"][lo:lo + 64, h // 2, t * P:(t + 1) * P],
                                       ikT[lo:lo + 64, 0:nk], start=True, stop=True)
                    mm.then_inc(full[r], 1)
                elif name == "scores":
                    kind, (t, h0, nh, nb) = CHUNKS[arg]
                    if arg == 0:
                        for s in (("proj", "uq0n"), ("proj", "uq1n"), ("proj", "kn0"), ("proj", "kn1"), ("qkpT", 0)):
                            wait_empty(pe, s)
                    if arg == 3:
                        wait_empty(pe, ("ropeT", "dk"))
                    if arg == 6:
                        wait_empty(pe, ("ropeT", "mk"))
                    if arg == 9:
                        wait_empty(pe, ("proj", "xq"))
                        wait_empty(pe, ("proj", "xk"))
                    may_fill(pe, key)
                    nk = nb * P
                    for i, hl in enumerate(slots(kind, nh)):
                        h = h0 + hl
                        dst = ps["A"][:, i * nk:(i + 1) * nk]
                        tt = slice(t * P, (t + 1) * P)
                        lo = 64 * (h % 2)
                        if kind == "mla":
                            pe.matmul(dst, qn[:, h, tt], kn[:, h, 0:nk], start=True, stop=False)
                            mm = pe.matmul(dst, qpeT[lo:lo + 64, h // 2, tt], kpeT[lo:lo + 64, 0:nk], start=False, stop=True)
                        elif kind == "cross":
                            mm = pe.matmul(dst, xqT[:, h, tt], xkT[:, h, 0:nk], start=True, stop=True)
                        else:
                            q, k = (qkT["mq"], qkT["mk"]) if kind == "moba" else (qkT["dq"], qkT["dk"])
                            mm = pe.matmul(dst, q[lo:lo + 64, h // 2, tt], k[lo:lo + 64, h // 2, 0:nk], start=True, stop=True)
                    mm.then_inc(full["A"], 1)
                elif name == "probsT":
                    pe.wait_ge(probs, SEQ[arg] + 1)
                    soft_sb = soft_1 if arg < 3 else soft_2
                    transposes(key, lambda i: soft_sb[:, SEQ[arg] % 2, i * P:(i + 1) * P], "B", 8)
                elif name == "pv":
                    kind, (t, h0, nh, nb) = CHUNKS[arg]
                    may_fill(pe, key)
                    if arg == 0:
                        wait_empty(pe, ("proj", "vm0"))
                        wait_empty(pe, ("proj", "vm1"))
                    if arg == 3:
                        wait_empty(pe, ("proj", "dv"))
                    if arg == 6:
                        wait_empty(pe, ("proj", "mv"))
                    if arg == 9:
                        wait_empty(pe, ("proj", "xv"))
                    prT = (prT_1 if arg < 3 else prT_2)[:, SEQ[arg] % 2]
                    for i, hl in enumerate(slots(kind, nh)):
                        h = h0 + hl
                        for b in range(nb):
                            if kind in ("mla", "cross"):
                                v = (vm if kind == "mla" else xv)[:, b, h * P:(h + 1) * P]
                                dst = ps["B"][:, hl * P:(hl + 1) * P]
                            else:
                                v = (dv if kind == "dsa" else mv)[:, b, h * 64:(h + 1) * 64]
                                dst = ps["B"][64 * (h % 2):64 * (h % 2) + 64, (hl // 2) * P:(hl // 2 + 1) * P]
                            mm = pe.matmul(dst, v, prT[:, i * nb + b, :], start=(b == 0), stop=(b == nb - 1))
                    mm.then_inc(full["B"], 1)
                elif name == "rank":
                    pe.wait_ge(rt_mask, 1)
                    may_fill(pe, key)
                    M = area(12, NT, 64, off=512)
                    z = ps["A"]
                    tri, one = consts[:, C_TRI:C_TRI + P], consts[:, C_ONE:C_ONE + P]
                    pe.matmul(z[:, 0:64], tri, M[:, 0, :], start=True, stop=True)
                    pe.matmul(z[:, 64:128], one, M[:, 0, :], start=True, stop=False)
                    pe.matmul(z[:, 64:128], tri, M[:, 1, :], start=False, stop=True)
                    pe.matmul(z[:, 128:192], one, M[:, 0, :], start=True, stop=False)
                    pe.matmul(z[:, 128:192], one, M[:, 1, :], start=False, stop=True).then_inc(full["A"], 1)
                elif name == "moe":
                    moe_tensor(pe)

        @block.scalar
        def _(act):
            n_seq = [0]

            def link(i):
                n_seq[0] += 1
                i.then_inc(act_seq, 1)
                act.wait_ge(act_seq, n_seq[0])

            act.dma_start(consts[:, :], ins["consts"]).then_inc(consts_in, 16)

            def col(dst, ap, k):
                act.dma_start(vec[:, dst:dst + k], ap, allow_slow_non_contiguous=True).then_inc(vec_in, 16)

            act.dma_start(ints[:, 0:2], ins["positions"][0].rearrange("(t p) -> p t", p=P),
                          allow_slow_non_contiguous=True).then_inc(vec_in, 16)
            kp = "(k p) -> p k"
            col(V_ATT, ins["attn_norm_w"][0].rearrange(kp, p=P), 8)
            col(V_FFN, ins["ffn_norm_w"][0].rearrange("(p k) -> p k", k=8), 8)
            col(V_IN2, ins["g_in_2"][0].rearrange(kp, p=P), 8)
            col(V_MEM, ins["g_mem_2"][0].rearrange(kp, p=P), 8)
            col(V_HGN, ins["hg_out_norm_w"][0].rearrange(kp, p=P), 1)
            col(V_LB0, ins["hg_lower_bound"][0].rearrange(kp, p=P), 8)
            col(V_LB1, ins["hg_lower_bound"][1].rearrange(kp, p=P), 8)
            col(V_QN, ins["mla_q_norm_w"][0].rearrange(kp, p=P), 3)
            col(V_KVN, ins["mla_kv_norm_w"][0].rearrange(kp, p=P), 2)
            col(V_BM, ins["b_merge_2"][0].rearrange(kp, p=P), 24)
            act.dma_start(rbias[:, 0:8], ins["router_group_b"].broadcast_to([P, 8])).then_inc(vec_in, 16)
            act.dma_start(rbias[:, 8:72], ins["router_expert_b"].broadcast_to([P, 64])).then_inc(vec_in, 16)

            def square_sums(src, junk, n, col, width):
                for t in range(NT):
                    i = act.activation(junk(t), src(t), ACT.Square, accum_out=small[:, col + t:col + t + 1])
                    if t == NT - 1:
                        link(i)
                act.activation(small[:, col + 2:col + 4], small[:, col:col + 2], ACT.Sqrt, bias=eps,
                               scale=1.0 / width).then_inc(roots, 1)

            def evac_copy(key, dst, region=None, view=None, func=ACT.Copy, **kw):
                r = region or region_of(key)
                act.wait_ge(full[r], USE[key][r])
                act.activation(dst, view(ps[r]), func, **kw).then_inc(empty[r], 1)

            four = lambda z: z[:, :].rearrange("p (c n) -> p c n", c=4)
            rows = lambda z: z[:, :].rearrange("p (t n) -> p t n", t=2)

            for name, arg, _ in PLAN:
                key = (name, arg)
                if name == "norm":
                    if arg == "x":
                        act.wait_ge(consts_in, 16)
                        act.wait_ge(x_in, 16)
                        square_sums(lambda t: X[:, t, :], lambda t: xn[:, t, :], 0, 0, D)
                        act.wait_ge(lb_diff, 1)
                        act.activation(vec[:, V_LB:V_LB + 8], vec[:, V_LB:V_LB + 8], ACT.Sigmoid).then_inc(lb_sig, 1)
                    elif arg == "ffn":
                        wait_empty(act, ("proj", "wo0"))
                        wait_empty(act, ("proj", "wo1"))
                        square_sums(lambda t: X[:, t, :], lambda t: xnf[:, t, :], 1, 8, D)
                    elif arg == "mem":
                        act.wait_ge(mem_in, 16)
                        wait_full(act, ("scores", 2))
                        square_sums(lambda t: mem[:, t, :], lambda t: memT[:, :, :].rearrange("p k s -> p (k s)")[:, t * D:(t + 1) * D], 2, 16, D)
                    elif arg == "mid":
                        act.wait_ge(added, rounds * (4 * GROUPS) + 1)
                        square_sums(lambda t: X[:, t, :], lambda t: xm[:, t, :], 3, 24, D)
                        act.wait_ge(stream_scaled, 1)
                        square_sums(lambda t: X[:, t, :], lambda t: xm[:, t, :], 3, 32, D)
                elif name == "proj":
                    if arg in ("hf0", "hf1"):
                        i = int(arg[2])
                        wait_full(act, key)
                        r = region_of(key)
                        if i == 0:
                            wait_full(act, ("norm", "x"))
                        act.activation(pre[:, 4 * i:4 * i + 4, :], four(ps[r]), ACT.Sigmoid).then_inc(empty[r], 1)
                    elif arg in ("hq0", "hq1"):
                        i = int(arg[2])
                        evac_copy(key, hq[:, 4 * i:4 * i + 4, :], view=four, func=ACT.Silu)
                    elif arg in ("hv0", "hv1"):
                        i = int(arg[2])
                        evac_copy(key, hv[:, :, 512 * i:512 * i + 512], view=rows)
                    elif arg in ("hg0", "hg1"):
                        i = int(arg[2])
                        evac_copy(key, GH[:, :, 512 * i:512 * i + 512], view=rows, func=ACT.Silu)
                    elif arg == "cl":
                        evac_copy(key, C[:, :, 0:512], view=rows)
                    elif arg == "ch":
                        evac_copy(key, C[:, :, 512:704], view=lambda z: rows(z)[:, :, 0:192])
                    elif arg[:2] in ("ga", "gb"):
                        i = int(arg[2])
                        evac_copy(key, (GA if arg[1] == "a" else GB)[:, 4 * i:4 * i + 4, :], view=four, func=ACT.Sigmoid)
                    elif arg in ("uq0n", "uq1n"):
                        i = int(arg[2])
                        if i == 0:
                            wait_full(act, ("level", len(LEVELS) + 1))
                        evac_copy(key, qn[:, 4 * i:4 * i + 4, :], view=four)
                    elif arg in ("kn0", "kn1"):
                        i = int(arg[2])
                        evac_copy(key, kn[:, 4 * i:4 * i + 4, :], view=four)
                    elif arg in ("vm0", "vm1"):
                        i = int(arg[2])
                        evac_copy(key, vm[:, :, 512 * i:512 * i + 512], view=rows)
                    elif arg in ("dv", "mv"):
                        evac_copy(key, dv[:, :, :] if arg == "dv" else mv[:, :, :], view=rows)
                    elif arg in ("dg", "mg", "xg"):
                        evac_copy(key, sg[arg][:, :, :], view=four, func=ACT.Silu)
                    elif arg == "xk":
                        evac_copy(key, xkT[:, :, :], view=four)
                    elif arg == "xq":
                        evac_copy(key, xqT[:, :, :], view=four)
                    elif arg == "xv":
                        evac_copy(key, xv[:, :, :], view=rows)
                    elif arg[:2] == "gl":
                        m = int(arg[2])
                        wait_full(act, key)
                        r = region_of(key)
                        for c in range(4):
                            i = act.activation(gl[m // 2][:, 4 * (m % 2) + c, :], ps[r][:, c * S:(c + 1) * S], ACT.Sigmoid,
                                               bias=vec[:, V_BM + 4 * m + c:V_BM + 4 * m + c + 1])
                        i.then_inc(empty[r], 1)
                elif name == "cnorm":
                    wait_empty(act, ("proj", "cl"))
                    wait_empty(act, ("proj", "ch"))
                    for t in range(NT):
                        for n, (a, b) in enumerate(((0, MLA_Q), (MLA_Q, MLA_Q + MLA_KV))):
                            i = act.activation(cT[:, 0:2, :].rearrange("p a b -> p (a b)")[:, 0:b - a], C[:, t, a:b], ACT.Square,
                                               accum_out=small[:, 40 + 2 * n + t:41 + 2 * n + t])
                            link(i)
                    act.activation(small[:, 44:46], small[:, 40:42], ACT.Sqrt, bias=eps, scale=1.0 / MLA_Q)
                    act.activation(small[:, 46:48], small[:, 42:44], ACT.Sqrt, bias=eps, scale=1.0 / MLA_KV).then_inc(roots, 1)
                    act.wait_ge(angles, 1)
                    act.activation(rope1[:, :, 0:32], rope1[:, :, 32:64], ACT.Sin).then_inc(sines, 1)
                elif name == "hg_out":
                    for t, r in enumerate("AB"):
                        act.wait_ge(full[r], USE[key][r])
                        act.activation(hgsq[:, t, :], ps[r][:, :], ACT.Square).then_inc(o_sq, 1)
                    act.wait_ge(o_summed, 1)
                    act.activation(small[:, 144:160], small[:, 128:144], ACT.Sqrt, bias=eps, scale=1.0 / P).then_inc(roots, 1)
                elif name == "qkpT":
                    for t, r in enumerate("AB"):
                        act.wait_ge(full[r], USE[key][r])
                        link(act.activation(qpeT[:, :, t * P:(t + 1) * P],
                                            ps[r][:, 0:512].rearrange("p (c n) -> p c n", c=4), ACT.Copy))
                        act.activation(kpeT[:, t * P:(t + 1) * P], ps[r][:, 512:640], ACT.Copy).then_inc(empty[r], 1)
                elif name == "ropeT":
                    for t, r in enumerate("AB"):
                        act.wait_ge(full[r], USE[key][r])
                        if arg == "ik":
                            act.activation(ikT[:, t * P:(t + 1) * P], ps[r][:, 0:P], ACT.Copy).then_inc(empty[r], 1)
                        else:
                            act.activation(qkT[arg][:, :, t * P:(t + 1) * P],
                                           ps[r][:, 0:512].rearrange("p (c n) -> p c n", c=4), ACT.Copy).then_inc(empty[r], 1)
                elif name == "index":
                    if arg >= 2:
                        act.wait_ge(index_added, arg - 1)
                    evac_copy(key, relu_s[:, arg % 2, :].rearrange("p (b n) -> p b n", b=2),
                              view=lambda z: rows(z)[:, :, 0:256], func=ACT.Relu, scale=64 ** -0.5)
                elif name == "soft":
                    g = arg
                    kind, (t, h0, nh, nb) = CHUNKS[g]
                    act.wait_ge(sm_max, SEQ[g] + 1)
                    nmax, sums, _ = chunk_stats(g)
                    nk = nb * P
                    sbuf = (soft_1 if g < 3 else soft_2)[:, SEQ[g] % 2]
                    for i in range(nh):
                        x = act.activation(sbuf[:, i * nk:(i + 1) * nk], sbuf[:, i * nk:(i + 1) * nk], ACT.Exp,
                                           bias=nmax[:, i:i + 1], accum_out=sums[:, i:i + 1])
                    x.then_inc(sm_exp, 1)
                elif name == "probsT":
                    g = arg
                    if SEQ[g] >= 2:
                        wait_full(act, ("pv", AT[SEQ[g] - 2]))
                    evac_copy(key, (prT_1 if g < 3 else prT_2)[:, SEQ[g] % 2],
                              view=lambda z: z[:, :].rearrange("p (b n) -> p b n", b=8))
                elif name == "rank":
                    act.wait_ge(rt_max, 1)
                    for t in range(NT):
                        x = act.activation(lrow[:, t, :], L[:, t, 0:8], ACT.Exp, bias=small[:, 208 + t:209 + t],
                                           accum_out=small[:, 210 + t:211 + t])
                    x.then_inc(rt_exp, 1)
                    act.wait_ge(rt_max2, 1)
                    act.activation(small[:, 214:216], small[:, 212:214], ACT.Exp).then_inc(rt_exp2, 1)
                elif name == "moe":
                    act.wait_ge(rounds_ready, 1)
                    rounds = act.value_load(ints[0:1, 2:3], min_val=0, max_val=S // CAP - 1) + 1
                    one_up(act, "act")
                    with act.Fori(0, rounds) as r:
                        for f in range(8):
                            act.wait_ge(selT_full, r * 8 + (f + 1))
                            act.activation(selT[:, 2 * f:2 * f + 2, :].rearrange("p g n -> p (g n)"),
                                           ps["B"][:, (f % 2) * 512:(f % 2 + 1) * 512], ACT.Copy).then_inc(selT_empty, 1)
                        with act.Fori(0, GROUPS) as g:
                            it = act.snap(r * GROUPS + g)
                            for j in range(EG):
                                act.wait_ge(hid_done, it * EG + j + 1)
                                act.wait_ge(products, it * NU + (MOE_AT[j, "w1"] + 1))
                                act.activation(gate_s[0:CAP, :], ps["P0"][0:CAP, 0:512], ACT.Silu).then_inc(silu_done, 1)
                            act.wait_ge(scattered, it * 4 + 1)
                            act.wait_ge(y_half, it + 1)
                            act.activation(ysb[:, 0:512], ps["P1"][:, 0:512], ACT.Copy).then_inc(y_copied, 1)
                            act.wait_ge(products, it * NU + NU)
                            act.activation(ysb[:, 512:1024], ps["P1"][:, 512:1024], ACT.Copy).then_inc(y_copied, 1)
                elif name == "final":
                    wait_empty(act, ("proj", "w20"))
                    wait_empty(act, ("proj", "w21"))
                    square_sums(lambda t: X[:, t, :], lambda t: xo[:, t, :], 4, 48, D)

        @block.vector
        def _(dve):
            n_seq = [0]

            def link(i):
                n_seq[0] += 1
                i.then_inc(dve_seq, 1)
                dve.wait_ge(dve_seq, n_seq[0])

            def tt(o, a, b, op):
                return dve.tensor_tensor(o, a, b, op)

            n_roots = [0]

            def inverse_root(col, n=2):
                n_roots[0] += 1
                dve.wait_ge(roots, n_roots[0])
                link(dve.reciprocal(small[:, col:col + n], small[:, col:col + n]))

            four = lambda z: z[:, :].rearrange("p (c n) -> p c n", c=4)
            rows = lambda z: z[:, :].rearrange("p (t n) -> p t n", t=2)

            def into_T(key, dst, wcol):
                for t, r in enumerate("AB"):
                    dve.wait_ge(full[r], USE[key][r])
                    tt(dst[:, :, t * P:(t + 1) * P], ps[r][:, :].rearrange("p (k n) -> p k n", k=KC),
                       bc(vec[:, wcol:wcol + KC], [P, KC, P], 2), ALU.mult).then_inc(empty[r], 1)

            def rope(z, heads, dst, tmp, cos, sin, release=None):
                zz = z.rearrange("p t (h d) -> p t h d", d=64)
                dd = dst.rearrange("p t (h d) -> p t h d", d=64)
                mm = tmp.rearrange("p t (h d) -> p t h d", d=64)
                shape = [P, heads, 32]
                for t in range(NT):
                    c = bc(cos[:, t, :], shape, 1)
                    s = bc(sin[:, t, :], shape, 1)
                    tt(dd[:, t, :, 0:32], zz[:, t, :, 0:32], c, ALU.mult)
                    tt(dd[:, t, :, 32:64], zz[:, t, :, 32:64], c, ALU.mult)
                    tt(mm[:, t, :, 0:32], zz[:, t, :, 32:64], s, ALU.mult)
                    x = tt(mm[:, t, :, 32:64], zz[:, t, :, 0:32], s, ALU.mult)
                if release:
                    r, n = release
                    x.then_inc(empty[r], 1)
                    dve.wait_ge(empty[r], n)
                else:
                    link(x)
                for t in range(NT):
                    tt(dd[:, t, :, 0:32], dd[:, t, :, 0:32], mm[:, t, :, 0:32], ALU.subtract)
                    x = tt(dd[:, t, :, 32:64], dd[:, t, :, 32:64], mm[:, t, :, 32:64], ALU.add)
                return x

            cos2 = consts[:, C_COS:C_COS + 64].rearrange("p (t i) -> p t i", t=2)
            sin2 = consts[:, C_SIN:C_SIN + 64].rearrange("p (t i) -> p t i", t=2)
            cos1, sin1 = rope1[:, 0:2, 0:32], rope1[:, 2:4, 0:32]

            def blocks(ap, b):
                return ap.rearrange("p h (n b) -> p (h n) b", b=2 * b)

            n_roped = [0]

            def signal_roped(i):
                n_roped[0] += 1
                i.then_inc(roped, 1)
                dve.wait_ge(roped, n_roped[0])

            for name, arg, _ in PLAN:
                key = (name, arg)
                if name == "norm" and arg == "x":
                    inverse_root(2)
                    for t in range(NT):
                        i = dve.tensor_scalar(xn[:, t, :], X[:, t, :], small[:, 2 + t:3 + t], None, ALU.mult)
                    i.then_inc(normed, 1)
                    dve.wait_ge(vec_in, 16 * 13)
                    into_T(key, hT, V_ATT)
                    tt(vec[:, V_LB:V_LB + 8], vec[:, V_LB0:V_LB0 + 8], vec[:, V_LB1:V_LB1 + 8], ALU.subtract).then_inc(lb_diff, 1)
                    ang = small[:, 256:320]
                    turn = small[:, 320:384]
                    link(dve.tensor_copy(small[:, 240:242], ints[:, 0:2]))
                    for t in range(NT):
                        i = dve.tensor_scalar(ang[:, 32 * t:32 * t + 32], consts[:, C_INVF:C_INVF + 32],
                                              small[:, 240 + t:241 + t], None, ALU.mult)
                    link(i)
                    magic = 1.5 * 2.0 ** 23
                    link(dve.tensor_scalar(turn, ang, float(1 / (2 * np.pi)), None, ALU.mult))
                    link(dve.tensor_scalar(turn, turn, magic, None, ALU.add))
                    link(dve.tensor_scalar(turn, turn, -magic, None, ALU.add))
                    c1 = 6.28125
                    c2 = float(np.float32(round((2 * np.pi - c1) * 2 ** 21) / 2 ** 21))
                    c3 = 2 * np.pi - c1 - c2
                    for c in (c1, c2, c3):
                        link(dve.scalar_tensor_tensor(out=ang, in0=turn, scalar=-float(c), in1=ang, op0=ALU.mult, op1=ALU.add))
                    top = float(np.nextafter(np.float32(np.pi), np.float32(0)))
                    link(dve.tensor_scalar(turn, ang, float(np.pi / 2), None, ALU.add))
                    wrap = small[:, 384:448]
                    link(dve.tensor_scalar(wrap, turn, float(np.pi), -2 * float(np.pi), ALU.is_gt, ALU.mult))
                    link(tt(turn, turn, wrap, ALU.add))
                    dve.tensor_scalar(rope1[:, 0:2, 32:64], turn.rearrange("p (t i) -> p t i", t=2), top, -top, ALU.min, ALU.max)
                    dve.tensor_scalar(rope1[:, 2:4, 32:64], ang.rearrange("p (t i) -> p t i", t=2), top, -top,
                                      ALU.min, ALU.max).then_inc(angles, 1)
                    dve.wait_ge(lb_sig, 1)
                    link(dve.tensor_scalar(vec[:, V_OML:V_OML + 8], vec[:, V_LB:V_LB + 8], -1.0, 1.0, ALU.mult, ALU.add))
                elif name == "norm" and arg == "ffn":
                    inverse_root(10)
                    for t in range(NT):
                        i = dve.tensor_scalar(xnf[:, t, :], X[:, t, :], small[:, 10 + t:11 + t], None, ALU.mult)
                    i.then_inc(normed, 1)
                    into_T(key, hT, V_FFN)
                elif name == "norm" and arg == "mem":
                    inverse_root(18)
                    for t in range(NT):
                        i = dve.tensor_scalar(mem[:, t, :], mem[:, t, :], small[:, 18 + t:19 + t], None, ALU.mult)
                    i.then_inc(normed, 1)
                    into_T(key, memT, V_MEM)
                elif name == "norm" and arg == "mid":
                    dve.wait_ge(added, rounds * (4 * GROUPS) + 1)
                    inverse_root(26)
                    dve.wait_ge(row_in, 16)
                    for t in range(NT):
                        i = dve.scalar_tensor_tensor(out=X[:, t, :], in0=X[:, t, :], scalar=small[:, 26 + t:27 + t],
                                                     in1=wrow, op0=ALU.mult, op1=ALU.mult)
                    i.then_inc(stream_scaled, 1)
                    dve.wait_ge(stream_scaled, 1)
                    inverse_root(34)
                    for t in range(NT):
                        i = dve.tensor_scalar(xm[:, t, :], X[:, t, :], small[:, 34 + t:35 + t], None, ALU.mult)
                    i.then_inc(normed, 1)
                    into_T(key, hT, V_IN2)
                elif name == "proj":
                    r = region_of(key)
                    if arg in ("hq0", "hq1"):
                        i = int(arg[2])
                        wait_empty(dve, ("proj", f"hf{i}"))
                        for h in range(4 * i, 4 * i + 4):
                            x = dve.tensor_scalar(pre[:, h, :], pre[:, h, :], vec[:, V_OML + h:V_OML + h + 1],
                                                  vec[:, V_LB + h:V_LB + h + 1], ALU.mult, ALU.add)
                        link(x)
                        dve.tensor_scalar(hk[:, 4 * i:4 * i + 4, :], pre[:, 4 * i:4 * i + 4, :], -1.0, 1.0, ALU.mult, ALU.add)
                        wait_empty(dve, key)
                        x = dve.tensor_scalar(hq[:, 4 * i:4 * i + 4, :], hq[:, 4 * i:4 * i + 4, :], HG_SCALE, None, ALU.mult)
                        if i:
                            x.then_inc(hg_ready, 1)
                    elif arg in ("uq0p", "uq1p"):
                        i = int(arg[2])
                        wait_full(dve, key)
                        if i == 0:
                            dve.wait_ge(sines, 1)
                            kz = C[:, :, 640:704]
                            link(rope(kz, 1, kpe2[:, :, 0:64], kpe2[:, :, 64:128], cos1, sin1))
                            signal_roped(dve.tensor_copy(kpe2[:, :, 64:128], kpe2[:, :, 0:64]))
                        x = rope(rows(ps[r])[:, :, 0:256], 4, qpe[:, :, 256 * i:256 * i + 256],
                                 qpeT[:, :, :].rearrange("p a b -> p (a b)")[:, 0:512].rearrange("p (t n) -> p t n", t=2),
                                 cos1, sin1, (r, USE[key][r]))
                        signal_roped(x)
                    elif arg in ("wa0", "wa1"):
                        i = int(arg[2])
                        wait_full(dve, key)
                        tt(Y[:, 4 * i:4 * i + 4, :], four(ps[r]), GA[:, 4 * i:4 * i + 4, :], ALU.mult).then_inc(empty[r], 1)
                    elif arg in ("wb0", "wb1"):
                        i = int(arg[2])
                        wait_full(dve, key)
                        link(tt(GB[:, 4 * i:4 * i + 4, :], four(ps[r]), GB[:, 4 * i:4 * i + 4, :], ALU.mult))
                        tt(Y[:, 4 * i:4 * i + 4, :], Y[:, 4 * i:4 * i + 4, :], GB[:, 4 * i:4 * i + 4, :], ALU.add).then_inc(empty[r], 1)
                    elif arg in ("wo0", "wo1", "w20", "w21"):
                        i = int(arg[2])
                        wait_full(dve, key)
                        x = tt(X[:, :, 512 * i:512 * i + 512], rows(ps[r]), X[:, :, 512 * i:512 * i + 512], ALU.add)
                        x.then_inc(empty[r], 1)
                    elif arg == "rt":
                        wait_full(dve, key)
                        dve.wait_ge(vec_in, 16 * 13)
                        for t in range(NT):
                            x = tt(L[:, t, :], ps[r][:, t * 512:t * 512 + 72], rbias[:, :], ALU.add)
                        x.then_inc(empty[r], 1)
                    elif arg == "ikw":
                        wait_full(dve, key)
                        z = rows(ps[r])
                        dve.tensor_scalar(iw[:, :, :], z[:, :, 64:72], 8 ** -0.5, None, ALU.mult)
                        link(rope(z[:, :, 0:64], 1, ikr[:, :, 0:64], ikr[:, :, 64:128], cos2, sin2, (r, USE[key][r])))
                        signal_roped(dve.tensor_copy(ikr[:, :, 64:128], ikr[:, :, 0:64]))
                    elif arg in ("iq", "dq", "dk", "mq", "mk"):
                        wait_full(dve, key)
                        prev = {"dq": "iq", "dk": "dq", "mq": "dk", "mk": "mq"}.get(arg)
                        if prev:
                            wait_full(dve, ("ropeT", prev))
                        signal_roped(rope(rows(ps[r]), 8, ropeA, ropeB, cos2, sin2, (r, USE[key][r])))
                    elif arg[0] == "u" and arg[1] in "mdx":
                        i = int(arg[2])
                        wait_full(dve, key)
                        g = {"m": 0, "d": 1, "x": 2}[arg[1]]
                        part = slice(4 * i, 4 * i + 4)
                        if g == 0:
                            for n in (0, 1):
                                wait_empty(dve, ("proj", f"gl{n}"))
                            tt(gl[0][:, part, :], four(ps[r]), gl[0][:, part, :], ALU.mult).then_inc(empty[r], 1)
                        else:
                            wait_empty(dve, ("proj", f"gl{2 * g + i}"))
                            link(tt(gl[g][:, part, :], four(ps[r]), gl[g][:, part, :], ALU.mult))
                            tt(gl[0][:, part, :], gl[0][:, part, :], gl[g][:, part, :], ALU.add).then_inc(empty[r], 1)
                elif name == "level":
                    n = arg
                    if n == 0:
                        link(dve.memset(hattn[:, :, :, :], 0.0))
                    if n <= len(LEVELS):
                        mask = bc(consts[:, C_LEV + P * n:C_LEV + P * (n + 1)].bitcast(I32), [P, HH, P], 1)
                        for t, r in enumerate("AB"):
                            dve.wait_ge(full[r], USE[key][r])
                            dve.copy_predicated(hattn[:, t, :, :], mask,
                                                ps[r][:, :].rearrange("p (h n) -> p h n", h=HH)).then_inc(empty[r], 1)
                    else:
                        wait_full(dve, key)
                        dve.tensor_copy(hattn[:, 2, :, :], ps["A"][:, :].rearrange("p (h n) -> p h n", h=HH)).then_inc(empty["A"], 1)
                    if n == 0:
                        link(dve.memset(suf[:, :, :], 1.0))
                        tt(lq[:, :, :], hq[:, :, :], pre[:, :, :], ALU.mult)
                        dve.tensor_copy(lk[:, :, :], hk[:, :, :]).then_inc(hg_ready, 1)
                    elif n <= len(LEVELS):
                        b = LEVELS[n - 1]
                        bs, bp = blocks(suf, b), blocks(pre, b)
                        cnt = HH * S // (2 * b)
                        link(tt(bs[:, :, 0:b], bs[:, :, 0:b], bp[:, :, 2 * b - 1:2 * b].broadcast_to([P, cnt, b]), ALU.mult))
                        link(tt(bp[:, :, b:2 * b], bp[:, :, b:2 * b], bp[:, :, b - 1:b].broadcast_to([P, cnt, b]), ALU.mult))
                        b *= 2
                        bs, bp = blocks(suf, b), blocks(pre, b)
                        tt(blocks(lq, b)[:, :, b:2 * b], blocks(hq, b)[:, :, b:2 * b], bp[:, :, b:2 * b], ALU.mult)
                        tt(blocks(lk, b)[:, :, 0:b], blocks(hk, b)[:, :, 0:b], bs[:, :, 0:b], ALU.mult).then_inc(hg_ready, 1)
                elif name == "cnorm":
                    inverse_root(44, 4)
                    for t in range(NT):
                        dve.tensor_scalar(C[:, t, 0:MLA_Q], C[:, t, 0:MLA_Q], small[:, 44 + t:45 + t], None, ALU.mult)
                        i = dve.tensor_scalar(C[:, t, MLA_Q:640], C[:, t, MLA_Q:640], small[:, 46 + t:47 + t], None, ALU.mult)
                    i.then_inc(normed, 1)
                    for t, r in enumerate("AB"):
                        dve.wait_ge(full[r], USE[key][r])
                        tt(cT[:, :, t * P:(t + 1) * P], ps[r][:, 0:640].rearrange("p (k n) -> p k n", k=5),
                           bc(vec[:, V_QN:V_QN + 5], [P, 5, P], 2), ALU.mult).then_inc(empty[r], 1)
                elif name == "hg_out":
                    for t in range(NT):
                        dve.wait_ge(o_sq, t + 1)
                        x = dve.tensor_reduce(small[:, 128 + 8 * t:136 + 8 * t],
                                              hgsq[:, t, :].rearrange("p (h n) -> p h n", h=HH), AX.X, ALU.add)
                    x.then_inc(o_summed, 1)
                    inverse_root(144, 16)
                    for n in (0, 1):
                        wait_empty(dve, ("proj", f"hg{n}"))
                    for t, r in enumerate("AB"):
                        o3 = hgo[:, t, :].rearrange("p (h n) -> p h n", h=HH)
                        tt(o3, ps[r][:, :].rearrange("p (h n) -> p h n", h=HH),
                           bc(small[:, 144 + 8 * t:152 + 8 * t], [P, HH, P], 2), ALU.mult).then_inc(empty[r], 1)
                        dve.wait_ge(empty[r], USE[key][r])
                        x = tt(hgo[:, t, :], hgo[:, t, :], GH[:, t, :], ALU.mult)
                    x.then_inc(o_done, 1)
                elif name == "hg_outT":
                    for t, r in enumerate("AB"):
                        dve.wait_ge(full[r], USE[key][r])
                        dve.tensor_scalar(oaT[:, :, t * P:(t + 1) * P], ps[r][:, :].rearrange("p (k n) -> p k n", k=KC),
                                          vec[:, V_HGN:V_HGN + 1], None, ALU.mult).then_inc(empty[r], 1)
                elif name == "index":
                    t, h0, nh = (0, 4 * arg, 4) if arg < 2 else (1, 2 * (arg - 2), 2)
                    nk = P * (t + 1)
                    dst = score[:, 0:P] if t == 0 else score[:, P:384]
                    wait_empty(dve, key)
                    for i in range(nh):
                        bank, at = index_at(i, nk)
                        src = relu_s[:, arg % 2, 256 * bank + at:256 * bank + at + nk]
                        w = iw[:, t, h0 + i:h0 + i + 1]
                        if h0 + i == 0:
                            x = dve.tensor_scalar(dst, src, w, None, ALU.mult)
                        else:
                            x = dve.scalar_tensor_tensor(out=dst, in0=src, scalar=w, in1=dst, op0=ALU.mult, op1=ALU.add)
                        if i < nh - 1:
                            link(x)
                    x.then_inc(index_added, 1)
                    dve.wait_ge(index_added, arg + 1)
                elif name == "topk":
                    link(tt(score[:, 0:P], score[:, 0:P], caus, ALU.add))
                    link(tt(score[:, 256:384], score[:, 256:384], caus, ALU.add))
                    for part, c in ((score[:, 0:P], 448), (score[:, P:384], 456)):
                        for _ in range(TOPK // 8):
                            top = small[:, c:c + 8]
                            link(dve.max(top, part))
                            link(dve.match_replace(part, top, part, USED))
                    link(dve.tensor_scalar(dmask[:, :], score[:, :], USED, NEG, ALU.not_equal, ALU.mult))
                    tt(dmask[:, 0:P], dmask[:, 0:P], caus, ALU.add)
                    link(tt(dmask[:, 256:384], dmask[:, 256:384], caus, ALU.add))
                elif name == "soft":
                    g = arg
                    kind, (t, h0, nh, nb) = CHUNKS[g]
                    nk = nb * P
                    nmax, sums, rsum = chunk_stats(g)
                    sbuf = (soft_1 if g < 3 else soft_2)[:, SEQ[g] % 2]
                    s3 = sbuf[:, 0:nh * nk].rearrange("p (h n) -> p h n", h=nh)
                    z3 = ps["A"][:, 0:nh * nk].rearrange("p (h n) -> p h n", h=nh)
                    scale = {"mla": MLA_SCALE, "dsa": 64 ** -0.5, "moba": 64 ** -0.5, "cross": 128 ** -0.5}[kind]
                    if SEQ[g] >= 2:
                        wait_full(dve, ("probsT", AT[SEQ[g] - 2]))
                    wait_full(dve, ("scores", g))
                    if g == 0:
                        wait_full(dve, ("hg_out", 0))
                    if kind == "cross":
                        x = dve.tensor_scalar(s3, z3, scale, None, ALU.mult)
                    elif kind == "dsa":
                        m = dmask[:, 0:P] if t == 0 else dmask[:, P:384]
                        x = dve.scalar_tensor_tensor(out=s3, in0=z3, scalar=scale, in1=bc(m, [P, nh, nk], 1), op0=ALU.mult, op1=ALU.add)
                    else:
                        if nb == 2:
                            dve.tensor_scalar(s3[:, :, 0:P], z3[:, :, 0:P], scale, None, ALU.mult)
                        x = dve.scalar_tensor_tensor(out=s3[:, :, nk - P:nk], in0=z3[:, :, nk - P:nk], scalar=scale,
                                                 in1=bc(caus, [P, nh, P], 1), op0=ALU.mult, op1=ALU.add)
                    x.then_inc(empty["A"], 1)
                    dve.wait_ge(empty["A"], USE["scores", g]["A"])
                    link(dve.tensor_reduce(rsum, s3, AX.X, ALU.max))
                    dve.tensor_scalar(nmax, rsum, -1.0, None, ALU.mult).then_inc(sm_max, 1)
                elif name == "normal":
                    g = arg
                    kind, (t, h0, nh, nb) = CHUNKS[g]
                    nk = nb * P
                    nmax, sums, rsum = chunk_stats(g)
                    s3 = (soft_1 if g < 3 else soft_2)[:, SEQ[g] % 2, 0:nh * nk].rearrange("p (h n) -> p h n", h=nh)
                    dve.wait_ge(sm_exp, SEQ[g] + 1)
                    link(dve.reciprocal(rsum, sums))
                    tt(s3, s3, bc(rsum, [P, nh, nk], 2), ALU.mult).then_inc(probs, 1)
                elif name == "pv":
                    g = arg
                    kind, (t, h0, nh, nb) = CHUNKS[g]
                    wait_full(dve, ("pv", g))
                    tsl = slice(t * P, (t + 1) * P)
                    if kind == "mla":
                        dve.tensor_copy(obT[:, h0:h0 + nh, tsl],
                                        ps["B"][:, 0:nh * P].rearrange("p (h n) -> p h n", h=nh)).then_inc(empty["B"], 1)
                    elif kind == "cross":
                        if t == 0:
                            wait_empty(dve, ("proj", "xg"))
                        tt(sg["xg"][:, :, tsl], ps["B"][:, 0:512].rearrange("p (h n) -> p h n", h=4),
                           sg["xg"][:, :, tsl], ALU.mult).then_inc(empty["B"], 1)
                    else:
                        gate = sg["dg" if kind == "dsa" else "mg"]
                        wait_empty(dve, ("proj", "dg" if kind == "dsa" else "mg"))
                        c0, n = h0 // 2, nh // 2
                        tt(gate[:, c0:c0 + n, tsl], ps["B"][:, 0:n * P].rearrange("p (h n) -> p h n", h=n),
                           gate[:, c0:c0 + n, tsl], ALU.mult).then_inc(empty["B"], 1)
                elif name == "rank":
                    route(dve, link, tt)
                elif name == "moe":
                    rounds = experts(dve, link, tt)
                elif name == "final":
                    wait_empty(dve, ("proj", "w20"))
                    wait_empty(dve, ("proj", "w21"))
                    inverse_root(50)
                    dve.wait_ge(row_in, 32)
                    for t in range(NT):
                        i = dve.scalar_tensor_tensor(out=xo[:, t, :], in0=X[:, t, :], scalar=small[:, 50 + t:51 + t],
                                                     in1=wrow_f, op0=ALU.mult, op1=ALU.mult)
                    i.then_inc(normed, 1)



_INS = ["x", "positions", "attn_norm_w", "w_in", "hg_lower_bound", "hg_out_norm_w", "mla_q_norm_w", "mla_w_uq",
        "mla_kv_norm_w", "mla_w_ukv", "w_branch_hgrn", "w_branch_mla", "w_out", "ffn_norm_w", "router_group_w",
        "router_group_b", "router_expert_w", "router_expert_b", "expert_w1", "expert_w3", "expert_w2",
        "final_norm_w", "mem_2", "g_in_2", "w_in_2", "b_merge_2", "g_mem_2", "w_mem_kv_2", "w_up_moba_2",
        "w_up_dsa_2", "w_up_cross_2", "w_out_2", "g_final_2"]


def kernel(**inputs):
    import concourse.bacc as bacc
    from concourse.bass_utils import run_bass_kernel_spmd

    nc = bacc.Bacc("TRN2", target_bir_lowering=False, num_devices=1)
    arrays, ins = {}, {}
    given = {name: np.ascontiguousarray(inputs[name]) for name in _INS}
    given["consts"] = shape_constants()
    for name, a in given.items():
        arrays[f"in_{name}"] = a
        ins[name] = nc.dram_tensor(f"in_{name}", a.shape, mybir.dt.from_np(a.dtype), kind="ExternalInput").ap()
    out = nc.dram_tensor("out_0", (1, S, D), F32, kind="ExternalOutput").ap()
    build(nc, ins, out)
    r = run_bass_kernel_spmd(nc, [arrays], core_ids=[0])
    return r.results[0]["out_0"]
```

```python
from contextlib import ExitStack

import numpy as np
import concourse.bass as bass
from concourse import mybir

F32 = mybir.dt.float32
F32R = mybir.dt.float32r
I32 = mybir.dt.int32
U32 = mybir.dt.uint32
ALU = mybir.AluOpType
ACT = mybir.ActivationFunctionType
AX = mybir.AxisListType

P = 128
S = 256
NT = S // P
D = 1024
KC = D // P
EPS = 1e-6
NEG = -1e30
USED = -3e38
SLOTS = 4
SLOT = 4096
HH = 8
XH = 4
HG_SCALE = 128 ** -0.5
MLA_Q, MLA_KV, MLA_ROPE = 384, 256, 64
MLA_SCALE = 192 ** -0.5
NG, NE_G, FF = 8, 8, 512
NEXP = NG * NE_G
CAP = 32
EG = 4
GROUPS = NEXP // EG
SEL = 128
TOPK = 64

LEVELS = [1, 2, 4, 8, 16, 32, 64]
C_ID, C_EPS, C_CAUS, C_LEV = 0, 128, 136, 264
C_TRI = C_LEV + 128 * (len(LEVELS) + 1)
C_ONE, C_IOTA, C_IOTA8, C_INVF, C_COS, C_SIN = (C_TRI + x for x in (128, 256, 288, 296, 328, 392))
NCONST = C_SIN + 64


def shape_constants():
    c = np.zeros((P, NCONST), np.float32)
    i = np.arange(P)
    row, col = i[:, None], i[None, :]
    c[:, C_ID:C_ID + P] = row == col
    c[:, C_CAUS:C_CAUS + P] = np.where(col <= row, 0.0, NEG)
    c[:, C_LEV:C_LEV + P] = row == col
    for n, b in enumerate(LEVELS):
        pair = (row // (2 * b) == col // (2 * b)) & (row % (2 * b) < b) & (col % (2 * b) >= b)
        c[:, C_LEV + P * (n + 1):C_LEV + P * (n + 2)] = pair
    c[:, C_TRI:C_TRI + P] = row < col
    c[:, C_ONE:C_ONE + P] = 1.0
    c[:, C_IOTA:C_IOTA + CAP] = np.arange(CAP)
    c[:, C_IOTA8:C_IOTA8 + 8] = np.arange(8)
    half = 32
    inv = (10000.0 ** (-np.arange(half, dtype=np.float64) / half)).astype(np.float32)
    c[:, C_INVF:C_INVF + half] = inv
    for t in range(NT):
        ang = ((i + t * P).astype(np.float32)[:, None] * inv).astype(np.float64)
        c[:, C_COS + half * t:C_COS + half * (t + 1)] = np.cos(ang)
        c[:, C_SIN + half * t:C_SIN + half * (t + 1)] = np.sin(ang)
    c[:, C_EPS] = EPS
    return c


def units_1():
    u = [(f"hf{i}", "w_in", 1024 + 512 * i, 512, 8) for i in range(2)]
    u += [(f"hq{i}", "w_in", 512 * i, 512, 8) for i in range(2)]
    u += [(f"hv{i}", "w_in", 2048 + 512 * i, 512, 8) for i in range(2)]
    u += [("cl", "w_in", 4096, 512, 8), ("ch", "w_in", 4608, 192, 8)]
    u += [(f"hg{i}", "w_in", 3072 + 512 * i, 512, 8) for i in range(2)]
    u += [(f"ga{i}", "w_in", 4800 + 512 * i, 512, 8) for i in range(2)]
    u += [(f"gb{i}", "w_in", 5824 + 512 * i, 512, 8) for i in range(2)]
    u += [("uq0", "mla_w_uq", 0, 768, 3), ("uq1", "mla_w_uq", 768, 768, 3), ("ukv", "mla_w_ukv", 0, 2048, 2)]
    u += [(f"wa{i}", "w_branch_hgrn", 512 * i, 512, 8) for i in range(2)]
    u += [(f"wb{i}", "w_branch_mla", 512 * i, 512, 8) for i in range(2)]
    u += [(f"wo{i}", "w_out", 512 * i, 512, 8) for i in range(2)]
    u += [("rt", "router", 0, 72, 8)]
    return u


def units_2():
    kv = [("xk", "w_mem_kv_2", 0, 512, 8), ("xv", "w_mem_kv_2", 512, 512, 8)]
    u = [("iq", 4096), ("ikw", 4608), ("dq", 2048), ("dv", 3072), ("dk", 2560), ("mv", 1024), ("mq", 0),
         ("dg", 3584), ("mk", 512), ("mg", 1536)]
    u = kv + [(n, "w_in_2", c, 72 if n == "ikw" else 512, 8) for n, c in u]
    u += [("xq", "w_in_2", 4680, 512, 8), ("xg", "w_in_2", 5192, 512, 8)]
    u += [(f"gl{i}", "w_in_2", 5704 + 512 * i, 512, 8) for i in range(6)]
    u += [("um", "w_up_moba_2", 0, 1024, 4), ("ud", "w_up_dsa_2", 0, 1024, 4), ("ux", "w_up_cross_2", 0, 1024, 4)]
    u += [(f"w2{i}", "w_out_2", 512 * i, 512, 8) for i in range(2)]
    return u


UNITS_1, UNITS_2 = units_1(), units_2()

CAUSAL = [(0, 0, 8, 1), (1, 0, 4, 2), (1, 4, 4, 2)]
CROSS = [(0, 0, 4, 2), (1, 0, 4, 2)]
CHUNKS = [("mla", c) for c in CAUSAL] + [("dsa", c) for c in CAUSAL] + [("moba", c) for c in CAUSAL] + \
         [("cross", c) for c in CROSS]


def slots(kind, nh):
    return list(range(nh)) if kind == "cross" else [*range(0, nh, 2), *range(1, nh, 2)]


def index_at(i, nk):
    return i % 2, (i // 2) * nk


def plan():
    p = []

    def proj(*names):
        p.extend(("proj", n, "P") for n in names)

    def soft(g):
        p.extend([("scores", g, "A"), ("soft", g, "")])

    def turn(g, following, *names, then=()):
        p.append(("normal", g, ""))
        if following is not None:
            soft(following)
        p.append(("probsT", g, "B"))
        p.extend((x, n, "") for x, n in then)
        proj(*names)
        p.append(("pv", g, "B"))

    p.append(("norm", "x", "AB"))
    proj("hf0", "hf1", "hq0", "hq1")
    p.append(("level", 0, "AB"))
    fill = [["hv0"], ["hv1"], ["cl"], ["ch"], ["hg0", "hg1"], ["ga0"], ["ga1"], ["gb0"]]
    for n in range(1, len(LEVELS) + 2):
        proj(*fill[n - 1])
        p.append(("level", n, "AB" if n <= len(LEVELS) else "A"))
    p.append(("cnorm", 0, "AB"))
    p.append(("hg_out", 0, "AB"))
    proj("gb1")
    proj("uq0n", "uq0p", "uq1n", "uq1p")
    p.append(("hg_outT", 0, "AB"))
    p.append(("qkpT", 0, "AB"))
    proj("kn0", "kn1")
    soft(0)
    proj("vm0", "vm1")
    turn(0, 1, "wa0")
    turn(1, 2, "wa1")
    p.append(("normal", 2, ""))
    p.append(("norm", "mem", "AB"))
    p.extend([("probsT", 2, "B"), ("pv", 2, "B")])
    proj("wb0", "wb1")
    proj("wo0", "wo1")
    p.append(("norm", "ffn", "AB"))
    proj("rt")
    p.append(("rank", 0, "A"))
    p.append(("moe", 0, ""))
    p.append(("stats", "mid", ""))
    proj("xk", "xv")
    p.append(("norm", "mid", "AB"))
    proj("iq", "ikw")
    p.append(("ropeT", "iq", "AB"))
    p.append(("ropeT", "ik", "AB"))
    proj("dq")
    p.extend([("index", 0, "A"), ("index", 1, "B")])
    proj("dv")
    p.append(("ropeT", "dq", "AB"))
    proj("dk")
    p.extend([("index", 2, "A"), ("index", 3, "B")])
    proj("mv")
    p.append(("ropeT", "dk", "AB"))
    proj("mq")
    p.extend([("index", 4, "A"), ("index", 5, "B")])
    proj("dg")
    p.append(("ropeT", "mq", "AB"))
    proj("mk", "mg")
    p.append(("ropeT", "mk", "AB"))
    soft(6)
    p.append(("topk", 0, ""))
    proj("xq")
    turn(6, 7, "xg", then=[("topk", 1)])
    turn(7, 8, "gl0", then=[("topk", 2), ("topk", 3)])
    turn(8, 3, "gl1")
    turn(3, 4, "gl2")
    turn(4, 5, "gl3")
    turn(5, 9, "gl4")
    turn(9, 10, "gl5")
    turn(10, None, "um0", "um1")
    proj("ud0", "ud1", "ux0", "ux1", "w20", "w21")
    p.append(("final", 0, ""))
    return p


PLAN = plan()
USE, FULL_AT = {}, {}


def count_uses():
    n = dict.fromkeys(("P0", "P1", "A", "B"), 0)
    turn = 0
    for name, arg, regions in PLAN:
        use = {}
        for r in regions:
            if r == "P":
                r, turn = f"P{turn}", 1 - turn
            n[r] += 1
            use[r] = n[r]
        USE[name, arg] = use


count_uses()

SEQ = {g: n for n, g in enumerate(arg for name, arg, _ in PLAN if name == "scores")}
AT = {n: g for g, n in SEQ.items()}

STEP_UNIT = {f"uq{i}{c}": f"uq{i}" for i in range(2) for c in "np"}
STEP_UNIT |= {n: "ukv" for n in ("kn0", "kn1", "vm0", "vm1")}
STEP_UNIT |= {f"u{c}{i}": f"u{c}" for c in "mdx" for i in range(2)}
LAST = {"uq0": "uq0p", "uq1": "uq1p", "ukv": "vm1", "um": "um1", "ud": "ud1", "ux": "ux1"}

MOE_UNITS = [(0, "w1"), (0, "w3"), (1, "w1"), (1, "w3"), (0, "w2"), (2, "w1"), (2, "w3"), (1, "w2"),
             (3, "w1"), (3, "w3"), (2, "w2"), (3, "w2")]
MOE_AT = {x: n for n, x in enumerate(MOE_UNITS)}
NU = len(MOE_UNITS)


def build(nc, ins, out):
    with ExitStack() as ctx:
        def sb(name, shape, dt=F32):
            return ctx.enter_context(nc.sbuf_tensor(name, shape, dt))

        def sem(name):
            return ctx.enter_context(nc.semaphore(name))

        ring = sb("ring", [P, SLOTS, SLOT])
        X = sb("X", [P, NT, D])
        consts = sb("consts_sb", [P, NCONST])
        arena = sb("arena", [P, 14 * 2048])
        small = sb("small", [P, 512])
        vec = sb("vec", [P, 128])
        rbias = sb("rbias", [P, 72])
        rope1 = sb("rope1", [P, 4, 64])
        idx8 = sb("idx8", [P, 8], U32)
        ints = sb("ints", [P, 4], I32)

        def area(a, *shape, off=0):
            n = int(np.prod(shape))
            ap = arena[:, a * 2048 + off:a * 2048 + off + n]
            if len(shape) == 1:
                return ap
            names = "abcd"[:len(shape)]
            kw = {names[i]: shape[i] for i in range(len(shape))}
            return ap.rearrange(f"p ({' '.join(names)}) -> p {' '.join(names)}", **kw)

        hT = area(12, KC, S)
        pre, suf, hq, hk = area(0, HH, S), area(1, HH, S), area(2, HH, S), area(3, HH, S)
        lq, lk, hv = area(4, HH, S), area(5, HH, S), area(6, NT, D)
        hattn = area(7, 3, HH, P)
        GA, GB, GH = area(9, KC, S), area(10, KC, S), area(11, NT, D)
        C = area(13, NT, 704)
        hgo, hgsq, oaT = area(4, NT, D), area(5, NT, D), area(2, KC, S)
        cT = sb("cT", [P, 5, S])
        kpe2 = sb("kpe2", [P, NT, P])
        kpeT = sb("kpeT", [P, S])
        qn, kn, vm = area(0, HH, S), area(1, HH, S), area(3, NT, D)
        qpe, qpeT = area(5, NT, 512), area(5, 4, S, off=1024)
        soft_1, prT_1 = area(6, 2, 1024), area(11, 2, 8, P)
        obT, Y = area(4, KC, S), area(7, KC, S)
        xn = area(0, NT, D)
        xnf = area(0, NT, D)
        arena_at = nc.lookup_mloc(arena).addr

        def halves(name, a, off, n):
            return nc.alloc_sbuf_tensor_at(name, [P, n], F32R, offset=arena_at + 4 * (2048 * a + off))

        wh = halves("w_high", 2, 0, 2 * SLOT)[:, :].rearrange("p (b n) -> p b n", b=2)
        wl = halves("w_low", 6, 0, 2 * SLOT)[:, :].rearrange("p (b n) -> p b n", b=2)
        xs = halves("x_halves", 10, 0, EG * KC * 2 * CAP + 2 * CAP)
        hs = halves("hid_halves", 10, 2112, 4 * 2 * CAP + 2 * CAP)
        GU = area(11, 2, FF, off=384)
        xg = area(11, KC, EG, CAP, off=384)
        gu_high, gu = area(11, 8, CAP, off=1408), area(11, 8, CAP, off=1664)
        hid = area(11, 4, CAP, off=1920)
        ysb = area(13, 2, D)
        selA = area(12, NT, EG, CAP, off=1088)
        selW = area(12, NT, EG, 2, CAP, off=1344)
        selTs = area(12, 2, S, off=0)
        L = area(12, NT, 72)
        lrow = area(12, NT, 8, off=256)
        PAD = NEXP + EG
        M, W, pos = area(12, NT, NEXP, off=512), area(12, NT, PAD, off=640), area(12, NT, PAD, off=776)
        memT = area(1, KC, S)
        mem = area(13, NT, D)
        xm, xo = area(0, NT, D), area(5, NT, D)
        qkT = {"iq": area(2, 4, S), "dq": area(2, 4, S, off=1024), "dk": area(3, 4, S),
               "mq": area(3, 4, S, off=1024), "mk": area(4, 4, S)}
        ikT = area(4, S, off=1024)
        ikr = area(4, NT, P, off=1280)
        iw = area(4, NT, 8, off=1536)
        dv, mv = area(5, NT, 512), area(5, NT, 512, off=1024)
        soft_2, prT_2 = area(6, 2, 1024), area(7, 2, 8, P)
        xqT, xkT, xv = area(8, 4, S), area(8, 4, S, off=1024), area(9, NT, 512)
        ropeA, ropeB = area(9, NT, 512, off=1024), area(13, NT, 512)
        relu_s = area(13, 2, 512, off=1024)
        score = sb("score", [P, 384])
        dmask = sb("dmask", [P, 384])
        sg = {"mg": area(10, 4, S), "dg": area(10, 4, S, off=1024), "xg": area(11, 4, S)}
        utmp = area(11, 4, S, off=1024)
        gl = [area(0, KC, S), area(1, KC, S), area(2, KC, S)]
        wrow, wrow_f = cT[:, 0:4, :].rearrange("p a b -> p (a b)"), area(13, D, off=1024)

        ps = {"P0": ctx.enter_context(nc.psum_tensor("psP0", [P, 1024], F32)),
              "P1": ctx.enter_context(nc.psum_tensor("psP1", [P, 1024], F32)),
              "A": ctx.enter_context(nc.psum_tensor("psA", [P, 1024], F32)),
              "B": ctx.enter_context(nc.psum_tensor("psB", [P, 1024], F32))}

        ident = consts[:, C_ID:C_ID + P]
        caus = consts[:, C_CAUS:C_CAUS + P]
        eps = consts[:, C_EPS:C_EPS + 1]

        V_ATT, V_FFN, V_IN2, V_MEM, V_HGN, V_LB0, V_LB1, V_LB, V_OML, V_QN, V_KVN, V_BM = (
            0, 8, 16, 24, 32, 40, 48, 56, 64, 72, 75, 80)

        full = {r: sem(f"full_{r}") for r in ps}
        empty = {r: sem(f"empty_{r}") for r in ps}
        landed = [sem(f"landed_{i}") for i in range(SLOTS)]
        landed2 = [sem(f"landed2_{i}") for i in range(SLOTS)]
        x_in, consts_in, vec_in, mem_in = sem("x_in"), sem("consts_in"), sem("vec_in"), sem("mem_in")
        masks_in = sem("masks_in")
        att_in = sem("att_in")
        row_in = sem("row_in")
        dve_seq, act_seq = sem("dve_seq"), sem("act_seq")
        squares, roots = sem("squares"), sem("roots")
        normed = sem("normed")
        lb_diff, lb_sig = sem("lb_diff"), sem("lb_sig")
        angles, sines = sem("angles"), sem("sines")
        hg_sig, hg_ready = sem("hg_sig"), sem("hg_ready")
        o_sq, o_done = sem("o_sq"), sem("o_done")
        sm_max, sm_exp, probs = sem("sm_max"), sem("sm_exp"), sem("probs")
        roped = sem("roped")
        relus = sem("relus")
        rt_max, rt_exp, rt_mask = sem("rt_max"), sem("rt_exp"), sem("rt_mask")
        rt_max2, rt_exp2 = sem("rt_max2"), sem("rt_exp2")
        rounds_ready = sem("rounds_ready")
        high_ready, low_ready = sem("high_ready"), sem("low_ready")
        products = sem("products")
        sel_ready, pos_step = sem("sel_ready"), sem("pos_step")
        selW_ready, selT_full, selT_copied = sem("selW_ready"), sem("selT_full"), sem("selT_copied")
        gathered, xg_step, xs_high, xs_ready = sem("gathered"), sem("xg_step"), sem("xs_high"), sem("xs_ready")
        g_copied, u_copied, turned = sem("g_copied"), sem("u_copied"), sem("turned")
        gu_high_copied, gu_summed, silu_done = sem("gu_high_copied"), sem("gu_summed"), sem("silu_done")
        no_rows = sem("no_rows")
        hid_step, y_copied, scattered, added = sem("hid_step"), sem("y_copied"), sem("scattered"), sem("added")
        o_summed, index_added = sem("o_summed"), sem("index_added")
        stream_scaled = sem("stream_scaled")
        ONE_UP = {"act": (g_copied, u_copied, y_copied), "dve": (pos_step,)}

        def one_up(e, name):
            for s in ONE_UP[name]:
                e.sem_inc(s, 1)
        stored = sem("stored")

        block = ctx.enter_context(nc.Block())

        def wait_full(e, key, region=None):
            for r, n in USE[key].items():
                if region in (None, r):
                    e.wait_ge(full[r], n)

        def wait_empty(e, key, region=None):
            for r, n in USE[key].items():
                if region in (None, r):
                    e.wait_ge(empty[r], n)

        def region_of(key):
            return list(USE[key])[0]

        def may_fill(e, key, region=None):
            for r, n in USE[key].items():
                if region in (None, r) and n > 1:
                    e.wait_ge(empty[r], n - 1)

        def bc(ap, shape, axis):
            return ap.unsqueeze(axis).broadcast_to(shape)

        unit_at = {}
        for lands, units in ((landed, UNITS_1), (landed2, UNITS_2)):
            for n, u in enumerate(units):
                loads = n // SLOTS + (0 if lands is landed2 and n % SLOTS < 2 else 1)
                unit_at[u[0]] = (n % SLOTS, lands[n % SLOTS], 16 * loads, u)
        n_rt = len(UNITS_1) - 1
        unit_at["rt"] = (n_rt % SLOTS, landed[n_rt % SLOTS], 16 * (n_rt // SLOTS) + 32, UNITS_1[n_rt])
        MOE_LAND = [16 * len([n for n in range(len(UNITS_1)) if n % SLOTS == s]) + (16 if s == n_rt % SLOTS else 0)
                    for s in range(SLOTS)]
        assert len(UNITS_1) % SLOTS == 0 and NU % SLOTS == 0

        def unit_ap(name):
            slot, _, _, (_, _, _, cols, kc) = unit_at[name]
            return ring[:, slot, 0:kc * cols].rearrange("p (k n) -> p k n", k=kc)

        def wait_unit(e, name):
            e.wait_ge(unit_at[name][1], unit_at[name][2])

        def chunk_stats(g):
            base = 64 + 24 * (SEQ[g] % 2)
            return [small[:, base + 8 * i:base + 8 * i + CHUNKS[g][1][2]] for i in range(3)]

        def half_count(it, n, h):
            return it * (2 * NU) + (2 * n + h + 1)

        def wait_moe_unit(e, it, n):
            e.wait_ge(landed[n % SLOTS], it * (16 * NU // SLOTS) + (MOE_LAND[n % SLOTS] + 16 * (n // SLOTS + 1)))

        def ring_half(n, h):
            return ring[:, n % SLOTS, h * 2048:(h + 1) * 2048]

        def w_half(w, n, h):
            return w[:, n % 2, h * 2048:(h + 1) * 2048]

        def split_high(act, it, n, h, first=False):
            if h == 0:
                wait_moe_unit(act, it, n)
            if not first:
                act.wait_ge(products, half_count(it, n - 2, h))
            act.activation(w_half(wh, n, h), ring_half(n, h), ACT.Copy).then_inc(high_ready, 1)

        def split_low(dve, it, n, h):
            dve.wait_ge(high_ready, half_count(it, n, h))
            dve.tensor_tensor(w_half(wl, n, h), ring_half(n, h), w_half(wh, n, h), ALU.subtract).then_inc(low_ready, 1)

        SCATTER = [(0, 0, ("A", 0)), (1, 0, ("B", 512)), (0, 1, ("A", 512)), (1, 1, ("A", 0))]

        def moe_tensor(pe):
            zG, zU = ps["P0"][:, 0:512], ps["P0"][:, 512:1024]
            zY, zA, zB = ps["P1"], ps["A"], ps["B"]

            def gather():
                for k in range(KC):
                    for t in range(NT):
                        mm = pe.matmul(zA[:, k * P:(k + 1) * P], xnf[:, t, k::KC],
                                       selA[:, t].rearrange("p j c -> p (j c)"), start=(t == 0), stop=(t == NT - 1))
                mm.then_inc(gathered, 1)

            def wait_halves(it, n, h):
                pe.wait_ge(high_ready, half_count(it, n, h))
                pe.wait_ge(low_ready, half_count(it, n, h))

            def up(it, j, which, z, copied):
                n = MOE_AT[j, which]
                if n == 0:
                    pe.wait_ge(xs_ready, it + 1)
                pe.wait_ge(copied, it * EG + (j + 1))
                for k in range(KC):
                    if k % 4 == 0:
                        wait_halves(it, n, k // 4)
                    for w in (wh, wl):
                        mm = pe.matmul(z, xs[:, (j * KC + k) * 64:(j * KC + k) * 64 + P],
                                       w[:, n % 2, k * 512:(k + 1) * 512],
                                       start=(k == 0 and w is wh), stop=(k == KC - 1 and w is wl))
                    if k % 4 == 3:
                        mm.then_inc(products, 1)

            def turn(it, j):
                if j == 0:
                    pe.wait_ge(added, it * 4 + 2)
                pe.wait_ge(g_copied, it * EG + (j + 1) + 1)
                pe.wait_ge(u_copied, it * EG + (j + 1) + 1)
                for i in range(8):
                    mm = pe.transpose(zB[:, i * P:(i + 1) * P], GU[:, i // 4, i % 4::4], ident)
                mm.then_inc(turned, 1)

            def down(it, j):
                n = MOE_AT[j, "w2"]
                pe.wait_ge(hid_step, it * (3 * EG) + (3 * j + 3))
                pe.wait_ge(y_copied, it * EG + (j + 1))
                for c in range(4):
                    if c % 2 == 0:
                        wait_halves(it, n, c // 2)
                    for w in (wh, wl):
                        for half in range(2):
                            mm = pe.matmul(zY[:, half * 512:(half + 1) * 512], hs[:, c * 64:c * 64 + P],
                                           w[:, n % 2, c * D + half * 512:c * D + (half + 1) * 512],
                                           start=(c == 0 and w is wh), stop=(c == 3 and w is wl))
                    if c % 2 == 1:
                        mm.then_inc(products, 1)

            def scatter(it, parts):
                for n in parts:
                    t, half, place = SCATTER[n]
                    r, c = place
                    if n == 3:
                        pe.wait_ge(added, it * 4 + 1)
                    for p in range(2):
                        mm = pe.matmul(ps[r][:, c:c + 512], selTs[:, p, t * P:(t + 1) * P],
                                       ysb[:, p, half * 512:(half + 1) * 512], start=(p == 0), stop=(p == 1))
                    mm.then_inc(scattered, 1)

            wait_empty(pe, ("rank", 0))
            wait_empty(pe, ("norm", "ffn"))
            wait_empty(pe, ("proj", "wo1"))
            wait_empty(pe, ("proj", "rt"))
            pe.wait_ge(rounds_ready, 1)
            rounds = pe.value_load(ints[0:1, 2:3], min_val=0, max_val=S // CAP - 1) + 1
            pe.wait_ge(sel_ready, 1)
            gather()
            pe.wait_ge(no_rows, 1)
            with pe.Fori(0, rounds) as r:
                with pe.Fori(0, GROUPS) as g:
                    it = pe.snap(r * GROUPS + g)
                    for n, (j, which) in enumerate(MOE_UNITS):
                        if which == "w1":
                            up(it, j, which, zG, g_copied)
                        elif which == "w3":
                            up(it, j, which, zU, u_copied)
                        else:
                            down(it, j)
                        if n == 0:
                            pe.wait_ge(y_copied, it * EG + 1)
                            scatter(it, (0, 1))
                        elif n == 1:
                            scatter(it, (2, 3))
                            turn(it, 0)
                        elif n == 3:
                            pe.wait_ge(selW_ready, it + 1)
                            pe.wait_ge(added, it * 4 + 4)
                            for t in range(NT):
                                for p in range(2):
                                    mm = pe.transpose(zA[:, (p * NT + t) * P:(p * NT + t + 1) * P],
                                                      selW[:, t, 2 * p:2 * p + 2].rearrange("p j h c -> p (j h c)"), ident)
                            mm.then_inc(selT_full, 1)
                        elif n in (4, 7, 10):
                            turn(it, j + 1)
                        if n == 10:
                            pe.wait_ge(sel_ready, it + 2)
                            pe.wait_ge(selT_copied, it + 1)
                            gather()
            pe.wait_ge(xs_ready, rounds * GROUPS + 1)
            pe.wait_ge(y_copied, rounds * (GROUPS * EG) + 1)
            scatter(pe.snap(rounds * GROUPS), range(4))
            return rounds

        def moe_scalar(act):
            act.wait_ge(rounds_ready, 1)
            rounds = act.value_load(ints[0:1, 2:3], min_val=0, max_val=S // CAP - 1) + 1
            one_up(act, "act")

            def split(it, *parts):
                for n, h in parts:
                    split_high(act, it, n, h)

            def copy_product(it, j, w):
                n = MOE_AT[j, ("w1", "w3")[w]]
                if j and w == 0:
                    act.wait_ge(turned, it * EG + j)
                act.wait_ge(products, half_count(it, n, 1))
                act.activation(GU[:, w, :], ps["P0"][:, w * 512:(w + 1) * 512], ACT.Copy).then_inc((g_copied, u_copied)[w], 1)

            def high_columns(it, j):
                act.wait_ge(turned, it * EG + (j + 1))
                act.activation(gu_high, ps["B"][:, :].rearrange("p (i n) -> p i n", i=8)[:, :, 0:CAP],
                               ACT.Copy).then_inc(gu_high_copied, 1)

            def silu(it, j):
                act.wait_ge(gu_summed, it * EG + (j + 1))
                act.activation(gu[:, 0:4, :], gu[:, 0:4, :], ACT.Silu).then_inc(silu_done, 1)

            def copy_y(it, j):
                act.wait_ge(products, half_count(it, MOE_AT[j, "w2"], 1))
                act.activation(ysb[64 * (j % 2):64 * (j % 2) + 64, j // 2, :], ps["P1"][0:64, :], ACT.Copy).then_inc(y_copied, 1)

            wait_full(act, ("proj", "rt"))
            for n in range(2):
                for h in range(2):
                    split_high(act, 0, n, h, first=True)
                if n == 0:
                    rows_high(act, 1)
            with act.Fori(0, rounds) as r:
                with act.Fori(0, GROUPS) as g:
                    it = act.snap(r * GROUPS + g)
                    split(it, (2, 0), (2, 1))
                    copy_product(it, 0, 0)
                    split(it, (3, 0), (3, 1))
                    copy_product(it, 0, 1)
                    high_columns(it, 0)
                    split(it, (4, 0))
                    silu(it, 0)
                    split(it, (4, 1))
                    copy_product(it, 1, 0)
                    split(it, (5, 0), (5, 1))
                    copy_product(it, 1, 1)
                    act.wait_ge(selT_full, it + 1)
                    act.activation(selTs.rearrange("p a n -> p (a n)"), ps["A"][:, 0:512], ACT.Copy).then_inc(selT_copied, 1)
                    split(it, (6, 0), (6, 1))
                    high_columns(it, 1)
                    copy_y(it, 0)
                    split(it, (7, 0))
                    silu(it, 1)
                    split(it, (7, 1))
                    copy_product(it, 2, 0)
                    split(it, (8, 0), (8, 1))
                    copy_product(it, 2, 1)
                    split(it, (9, 0), (9, 1))
                    high_columns(it, 2)
                    copy_y(it, 1)
                    split(it, (10, 0))
                    silu(it, 2)
                    split(it, (10, 1))
                    copy_product(it, 3, 0)
                    split(it, (11, 0), (11, 1))
                    copy_product(it, 3, 1)
                    split(it, (12, 0), (12, 1))
                    high_columns(it, 3)
                    copy_y(it, 2)
                    silu(it, 3)
                    rows_high(act, it + 2)
                    split(it, (13, 0), (13, 1))
                    copy_y(it, 3)
            return rounds

        def rows_high(act, n):
            act.wait_ge(xg_step, n)
            act.activation(x_half(0), xg, ACT.Copy).then_inc(xs_high, 1)

        def x_half(h):
            return xs[:, 0:EG * KC * 64].rearrange("p (j k h c) -> p k j h c", j=EG, k=KC, h=2)[:, :, :, h, :]

        def h_half(h):
            return hs[:, 0:4 * 64].rearrange("p (k h c) -> p k h c", k=4, h=2)[:, :, h, :]

        def route(dve, link, tt):
            iota8 = consts[:, C_IOTA8:C_IOTA8 + 8]
            wait_empty(dve, ("proj", "rt"))
            oneG, one0, one1 = (area(12, NT, 8, off=o) for o in (320, 336, 352))
            esel = area(12, NT, 8, off=368)
            m8 = area(12, NT, 8, off=384)
            m8b = area(12, NT, 8, off=400)
            fidx = area(12, NT, off=416)
            prod = area(12, 64, off=1024)

            def first_of(row, top, t):
                link(dve.max(top, row))
                link(dve.max_index(idx8[:, :], top, row))
                link(dve.tensor_copy(fidx[:, t:t + 1], idx8[:, 0:1]))

            for t in range(NT):
                first_of(L[:, t, 0:8], m8[:, t, :], t)
                link(dve.tensor_scalar(oneG[:, t, :], iota8, fidx[:, t:t + 1], None, ALU.is_equal))
            dve.tensor_scalar(small[:, 208:210].unsqueeze(2), m8[:, :, 0:1], -1.0, None, ALU.mult).then_inc(rt_max, 1)
            for t in range(NT):
                p3 = prod.rearrange("p (e g) -> p e g", g=8)
                link(tt(p3, L[:, t, 8:72].rearrange("p (g e) -> p e g", g=8), bc(oneG[:, t, :], [P, 8, 8], 1), ALU.mult))
                link(dve.tensor_reduce(esel[:, t, :], p3, AX.X, ALU.add))
                first_of(esel[:, t, :], m8[:, t, :], t)
                link(dve.tensor_scalar(one0[:, t, :], iota8, fidx[:, t:t + 1], None, ALU.is_equal))
                link(dve.scalar_tensor_tensor(out=esel[:, t, :], in0=one0[:, t, :], scalar=USED, in1=esel[:, t, :],
                                              op0=ALU.mult, op1=ALU.add))
                first_of(esel[:, t, :], m8b[:, t, :], t)
                link(dve.tensor_scalar(one1[:, t, :], iota8, fidx[:, t:t + 1], None, ALU.is_equal))
            tt(small[:, 212:214].unsqueeze(2), m8b[:, :, 0:1], m8[:, :, 0:1], ALU.subtract).then_inc(rt_max2, 1)
            link(tt(esel[:, :, :], one0[:, :, :], one1[:, :, :], ALU.add))
            for t in range(NT):
                i = tt(M[:, t, :].rearrange("p (g e) -> p g e", g=8), bc(oneG[:, t, :], [P, 8, 8], 2),
                       bc(esel[:, t, :], [P, 8, 8], 1), ALU.mult)
            i.then_inc(rt_mask, 1)
            dve.wait_ge(rt_exp, 1)
            dve.wait_ge(rt_exp2, 1)
            gw, e2 = small[:, 210:212], small[:, 214:216]
            link(dve.tensor_scalar(small[:, 216:218], e2, 1.0, None, ALU.add))
            link(tt(small[:, 216:218], small[:, 216:218], gw, ALU.mult))
            link(dve.reciprocal(small[:, 216:218], small[:, 216:218]))
            link(tt(small[:, 218:220], small[:, 216:218], e2, ALU.mult))
            for t in range(NT):
                link(dve.tensor_scalar(one0[:, t, :], one0[:, t, :], small[:, 216 + t:217 + t], None, ALU.mult))
                link(dve.scalar_tensor_tensor(out=one1[:, t, :], in0=one1[:, t, :], scalar=small[:, 218 + t:219 + t],
                                              in1=one0[:, t, :], op0=ALU.mult, op1=ALU.add))
                link(tt(W[:, t, 0:NEXP].rearrange("p (g e) -> p g e", g=8), bc(oneG[:, t, :], [P, 8, 8], 2),
                        bc(one1[:, t, :], [P, 8, 8], 1), ALU.mult))
            wait_full(dve, ("rank", 0))
            z = ps["A"]
            link(dve.tensor_copy(W[:, :, NEXP:PAD], W[:, :, 0:EG]))
            p3 = pos[:, :, 0:NEXP]
            link(dve.tensor_scalar(p3, z[:, 0:128].rearrange("p (t e) -> p t e", t=NT), 1.0, None, ALU.add))
            link(tt(p3, p3, M, ALU.mult))
            link(dve.tensor_scalar(p3, p3, -1.0, None, ALU.add))
            link(dve.tensor_scalar(pos[:, :, NEXP:PAD], pos[:, :, 0:EG], -float(CAP), None, ALU.add))
            link(dve.tensor_reduce(small[:, 220:221], z[:, 128:192], AX.X, ALU.max))
            link(dve.tensor_scalar(small[:, 220:221], small[:, 220:221], -float(CAP), None, ALU.add))
            link(dve.tensor_scalar(small[:, 224:232], iota8, float(CAP), small[:, 220:221], ALU.mult, ALU.is_lt))
            link(dve.tensor_reduce(small[:, 221:222], small[:, 224:232], AX.X, ALU.add))
            dve.tensor_copy(ints[:, 2:3], small[:, 221:222]).then_inc(rounds_ready, 1)
            dve.wait_ge(rounds_ready, 1)
            link(dve.memset(xs[:, EG * KC * 64:EG * KC * 64 + 64].bitcast(F32), 0.0))
            dve.memset(hs[:, 256:320].bitcast(F32), 0.0).then_inc(empty["A"], 1)

        def experts(dve, link, tt):
            iota = consts[:, C_IOTA:C_IOTA + CAP].unsqueeze(1).unsqueeze(1).broadcast_to([P, NT, EG, CAP])
            rounds = dve.value_load(ints[0:1, 2:3], min_val=0, max_val=S // CAP - 1) + 1
            one_up(dve, "dve")

            def split(it, *parts):
                for n, h in parts:
                    split_low(dve, it, n, h)

            def select(columns):
                p4 = pos[:, :, columns].unsqueeze(3).broadcast_to([P, NT, EG, CAP])
                tt(selA, iota, p4, ALU.is_equal).then_inc(sel_ready, 1)

            def rows(n):
                dve.wait_ge(gathered, n)
                tt(xg.rearrange("p k j c -> p k (j c)"), ps["A"][:, :].rearrange("p (k n) -> p k n", k=KC),
                   bc(vec[:, V_FFN:V_FFN + KC], [P, KC, SEL], 2), ALU.mult).then_inc(xg_step, 1)
                dve.wait_ge(xs_high, n)
                tt(x_half(1), xg, x_half(0), ALU.subtract).then_inc(xs_ready, 1)

            def sum_columns(it, j):
                dve.wait_ge(gu_high_copied, it * EG + (j + 1))
                tt(gu, gu_high, ps["B"][:, :].rearrange("p (i n) -> p i n", i=8)[:, :, CAP:2 * CAP],
                   ALU.add).then_inc(gu_summed, 1)

            def hidden(it, j):
                dve.wait_ge(silu_done, it * EG + (j + 1))
                tt(hid, gu[:, 0:4, :], gu[:, 4:8, :], ALU.mult).then_inc(hid_step, 1)
                dve.wait_ge(hid_step, it * (3 * EG) + (3 * j + 1))
                dve.tensor_copy(h_half(0), hid).then_inc(hid_step, 1)
                dve.wait_ge(hid_step, it * (3 * EG) + (3 * j + 2))
                tt(h_half(1), hid, h_half(0), ALU.subtract).then_inc(hid_step, 1)

            def add(it, *parts):
                for n in parts:
                    t, half, (reg, c) = SCATTER[n]
                    dve.wait_ge(scattered, it * 4 + (n + 1))
                    dst = X[:, t, half * 512:(half + 1) * 512]
                    tt(dst, dst, ps[reg][:, c:c + 512], ALU.add).then_inc(added, 1)

            select(slice(0, EG))
            split(0, (0, 0), (0, 1))
            rows(1)
            split(0, (1, 0), (1, 1))
            with dve.Fori(0, rounds) as r:
                with dve.Fori(0, GROUPS) as g:
                    it = dve.snap(r * GROUPS + g)
                    split(it, (2, 0), (2, 1))
                    add(it, 0, 1)
                    dve.wait_ge(sel_ready, it + 1)
                    w4 = W[:, :, bass.ds(g * EG, EG)].unsqueeze(3).broadcast_to([P, NT, EG, CAP])
                    tt(selW[:, :, :, 0, :], selA, w4, ALU.mult)
                    tt(selW[:, :, :, 1, :], selA, w4, ALU.mult).then_inc(selW_ready, 1)
                    split(it, (3, 0), (3, 1))
                    dve.wait_ge(selW_ready, it + 1)
                    dve.wait_ge(pos_step, r + 1)
                    select(bass.ds(g * EG + EG, EG))
                    add(it, 2, 3)
                    sum_columns(it, 0)
                    split(it, (4, 0))
                    hidden(it, 0)
                    split(it, (4, 1), (5, 0), (5, 1), (6, 0), (6, 1))
                    sum_columns(it, 1)
                    split(it, (7, 0))
                    hidden(it, 1)
                    split(it, (7, 1), (8, 0), (8, 1), (9, 0), (9, 1))
                    sum_columns(it, 2)
                    split(it, (10, 0))
                    hidden(it, 2)
                    split(it, (10, 1), (11, 0), (11, 1), (12, 0), (12, 1))
                    sum_columns(it, 3)
                    hidden(it, 3)
                    rows(it + 2)
                    split(it, (13, 0), (13, 1))
                dve.wait_ge(sel_ready, r * GROUPS + (GROUPS + 1))
                dve.tensor_scalar(pos, pos, -float(CAP), None, ALU.add).then_inc(pos_step, 1)
            add(dve.snap(rounds * GROUPS), 0, 1, 2, 3)
            return rounds

        @block.sync
        def _(sp):
            for t in range(NT):
                sp.dma_start(X[:, t, :], ins["x"][0][t * P:(t + 1) * P, :]).then_inc(x_in, 16)

            def load(units, n):
                name, tensor, c0, cols, kc = units[n]
                if n >= SLOTS:
                    prev = units[n - SLOTS][0]
                    key = ("proj", LAST.get(prev, prev))
                    r = region_of(key)
                    sp.wait_ge(full[r], USE[key][r])
                slot, land, _, _ = unit_at[name]
                dst = ring[:, slot, 0:kc * cols].rearrange("p (k n) -> p k n", k=kc)
                if name == "rt":
                    sp.dma_start(dst[:, :, 0:8], ins["router_group_w"][0].rearrange("(p k) n -> p k n", k=KC)).then_inc(land, 16)
                    sp.dma_start(dst[:, :, 8:72], ins["router_expert_w"][0].rearrange("(p k) n -> p k n", k=KC)).then_inc(land, 16)
                    return
                src = ins[tensor][0][:, c0:c0 + cols].rearrange("(k p) n -> p k n", p=P)
                if units is UNITS_2 and n < 2:
                    land = landed[slot]
                sp.dma_start(dst, src).then_inc(land, 16)

            for n in range(len(UNITS_1)):
                if UNITS_1[n][0] == "wb0":
                    wait_full(sp, ("cnorm", 0))
                    sp.wait_ge(roped, 1)
                    sp.dma_start(mem[:, :, :], ins["mem_2"][0].rearrange("(t p) d -> p t d", p=P)).then_inc(mem_in, 16)
                load(UNITS_1, n)
            wait_full(sp, ("proj", "wb1"))
            sp.dma_start(wrow, ins["final_norm_w"].unsqueeze(0).broadcast_to([P, D])).then_inc(row_in, 16)

            ew = {"w1": ins["expert_w1"][0].rearrange("e (p k) n -> e p (k n)", k=KC),
                  "w3": ins["expert_w3"][0].rearrange("e (p k) n -> e p (k n)", k=KC),
                  "w2": ins["expert_w2"][0].rearrange("e (p k) n -> e p (k n)", k=4)}

            def group_loads(r, g, peeled):
                for n, (j, which) in enumerate(MOE_UNITS):
                    if peeled and n < SLOTS:
                        prev = UNITS_1[len(UNITS_1) - SLOTS + n][0]
                        key = ("proj", LAST.get(prev, prev))
                        reg = region_of(key)
                        sp.wait_ge(full[reg], USE[key][reg])
                    else:
                        sp.wait_ge(low_ready, r * (2 * GROUPS * NU) + g * (2 * NU) + 2 * (n - SLOTS + 1))
                    src = ew[which][j] if peeled else ew[which][bass.ds(g * EG + j, 1)].rearrange("e p n -> p (e n)")
                    sp.dma_start(ring[:, n % SLOTS, :], src).then_inc(landed[n % SLOTS], 16)

            group_loads(0, 0, True)
            with sp.Fori(1, GROUPS) as g:
                group_loads(0, g, False)
            sp.wait_ge(rounds_ready, 1)
            rounds = sp.value_load(ints[0:1, 2:3], min_val=0, max_val=S // CAP - 1) + 1
            with sp.If(rounds > 1):
                with sp.Fori(1, rounds) as r:
                    with sp.Fori(0, GROUPS) as g:
                        group_loads(r, g, False)
            for n in range(len(UNITS_2)):
                if n < SLOTS:
                    sp.wait_ge(low_ready, rounds * (2 * GROUPS * NU) - 2 * (SLOTS - 1 - n))
                if UNITS_2[n][0] == "um":
                    sp.wait_ge(index_added, 6)
                    sp.dma_start(wrow_f, ins["g_final_2"].unsqueeze(0).broadcast_to([P, D])).then_inc(row_in, 16)
                load(UNITS_2, n)
            sp.wait_ge(normed, 6)
            sp.dma_start(out[0].rearrange("(t p) d -> p t d", p=P), xo[:, :, :]).then_inc(stored, 16)
            sp.wait_ge(stored, 16)

        @block.gpsimd
        def _(pool):
            pool.wait_ge(rounds_ready, 1)
            pool.memset(selTs, 0.0)
            pool.memset(ysb, 0.0).then_inc(no_rows, 1)

        @block.tensor
        def _(pe):
            def transposes(key, src_of, region, n, done=True):
                may_fill(pe, key, region)
                for i in range(n):
                    mm = pe.transpose(ps[region][:, i * P:(i + 1) * P], src_of(i), ident)
                mm.then_inc(full[region], 1)

            def proj(key, name, lhs_of, rhs_of, kc, outs):
                may_fill(pe, key)
                r = region_of(key)
                for o in range(len(outs(ps[r]))):
                    dst = outs(ps[r])[o]
                    for k in range(kc):
                        mm = pe.matmul(dst, lhs_of(o, k), rhs_of(o, k), start=(k == 0), stop=(k == kc - 1))
                mm.then_inc(full[r], 1)

            def rows_out(cols):
                return lambda z: [z[:, t * 512:t * 512 + cols] for t in range(NT)]

            def feats_out(z):
                return [z[:, c * S:(c + 1) * S] for c in range(4)]

            def feature_major(key, name, src, kc=8, c0=0, stride=P):
                w = unit_ap(STEP_UNIT.get(name, name))
                proj(key, name, lambda o, k: w[:, k, c0 + o * stride:c0 + o * stride + P],
                     lambda o, k: src[:, k, :], kc, feats_out)

            def token_major(key, name, src, kc=8, w=None, cols=512):
                w = unit_ap(name) if w is None else w
                proj(key, name, lambda o, k: src[:, k, o * P:(o + 1) * P],
                     lambda o, k: w[:, k], kc, rows_out(cols))

            rope_n = {"iq": 1, "ik": 1, "dq": 2, "dk": 3, "mq": 4, "mk": 5}

            for name, arg, _ in PLAN:
                key = (name, arg)
                if name == "norm":
                    if arg == "x":
                        pe.wait_ge(consts_in, 16)
                    pe.wait_ge(normed, {"x": 1, "mem": 3, "ffn": 4, "mid": 5}[arg])
                    src = {"x": xn, "ffn": xnf, "mem": mem, "mid": xm}[arg]
                    for t, r in enumerate("AB"):
                        pick = (lambda i, t=t: src[:, t, i::KC]) if arg == "ffn" else \
                               (lambda i, t=t: src[:, t, i * P:(i + 1) * P])
                        transposes(key, pick, r, KC)
                elif name == "proj":
                    unit = STEP_UNIT.get(arg, arg)
                    if unit in (UNITS_2[0][0], UNITS_2[1][0]):
                        n = unit_at[unit][0]
                        pe.wait_ge(landed[n], rounds * (GROUPS * 16 * NU // SLOTS) + (MOE_LAND[n] + 16))
                    else:
                        wait_unit(pe, unit)
                    if arg == "hf0":
                        wait_empty(pe, ("norm", "x"))
                    if arg in ("hf0", "hf1", "hq0", "hq1", "ga0", "ga1", "gb0", "gb1"):
                        feature_major(key, arg, hT)
                    elif arg in ("hv0", "hv1", "hg0", "hg1", "cl"):
                        token_major(key, arg, hT)
                    elif arg == "ch":
                        token_major(key, arg, hT, cols=192)
                    elif arg in ("uq0n", "uq1n"):
                        if arg == "uq0n":
                            wait_empty(pe, ("cnorm", 0))
                        feature_major(key, arg, cT, kc=3, stride=192)
                    elif arg in ("uq0p", "uq1p"):
                        w = ring[:, unit_at[unit][0], 0:3 * 768].rearrange("p (k h c) -> p k h c", k=3, h=4)[:, :, :, P:192]
                        token_major(key, arg, cT, kc=3, w=w, cols=256)
                    elif arg in ("kn0", "kn1"):
                        feature_major(key, arg, cT[:, 3:5, :], kc=2, c0=1024 * int(arg[2]), stride=256)
                    elif arg in ("vm0", "vm1"):
                        i = int(arg[2])
                        w = ring[:, unit_at[unit][0], :].rearrange("p (k h c) -> p k h c", k=2, h=8)[:, :, 4 * i:4 * i + 4, P:256]
                        token_major(key, arg, cT[:, 3:5, :], kc=2, w=w)
                    elif arg in ("wa0", "wa1"):
                        if arg == "wa0":
                            wait_empty(pe, ("hg_outT", 0))
                        feature_major(key, arg, oaT)
                    elif arg in ("wb0", "wb1"):
                        if arg == "wb0":
                            wait_empty(pe, ("pv", 2))
                        feature_major(key, arg, obT)
                    elif arg in ("wo0", "wo1"):
                        if arg == "wo0":
                            wait_empty(pe, ("proj", "wb0"))
                            wait_empty(pe, ("proj", "wb1"))
                        token_major(key, arg, Y)
                    elif arg == "rt":
                        wait_empty(pe, ("norm", "ffn"))
                        token_major(key, arg, hT, cols=72)
                    elif arg in ("iq", "dq", "dk", "dv", "mq", "mk", "mv"):
                        if arg == "iq":
                            wait_empty(pe, ("norm", "mid"))
                        token_major(key, arg, hT)
                    elif arg == "ikw":
                        token_major(key, arg, hT, cols=72)
                    elif arg in ("xq", "mg", "dg", "xg") or arg[:2] == "gl":
                        feature_major(key, arg, hT)
                    elif arg == "xk":
                        wait_empty(pe, ("norm", "mem"))
                        feature_major(key, arg, memT)
                    elif arg == "xv":
                        token_major(key, arg, memT)
                    elif arg[0] == "u":
                        kind = {"m": "mg", "d": "dg", "x": "xg"}[arg[1]]
                        last = {"m": 8, "d": 5, "x": 10}[arg[1]]
                        if arg[2] == "0":
                            wait_empty(pe, ("pv", last))
                        feature_major(key, arg, sg[kind], kc=4, c0=512 * int(arg[2]))
                    elif arg in ("w20", "w21"):
                        if arg == "w20":
                            wait_empty(pe, ("proj", "ux0"))
                            wait_empty(pe, ("proj", "ux1"))
                        token_major(key, arg, gl[0])
                elif name == "level":
                    n = arg
                    if n:
                        pe.wait_ge(hg_ready, n + 1)
                    else:
                        pe.wait_ge(hg_ready, 1)
                    q, k = (lq, lk) if n else (hq, hk)
                    if n <= len(LEVELS):
                        for t, r in enumerate("AB"):
                            may_fill(pe, key, r)
                            for h in range(HH):
                                mm = pe.matmul(ps[r][:, h * P:(h + 1) * P], k[:, h, t * P:(t + 1) * P],
                                               q[:, h, t * P:(t + 1) * P], start=True, stop=True)
                            mm.then_inc(full[r], 1)
                    else:
                        may_fill(pe, key)
                        for h in range(HH):
                            mm = pe.matmul(ps["A"][:, h * P:(h + 1) * P], k[:, h, 0:P], q[:, h, P:S],
                                           start=True, stop=True)
                        mm.then_inc(full["A"], 1)
                elif name == "cnorm":
                    pe.wait_ge(normed, 2)
                    for t, r in enumerate("AB"):
                        transposes(key, lambda i, t=t: C[:, t, i * P:(i + 1) * P], r, 5)
                elif name == "hg_out":
                    wait_empty(pe, ("proj", "hv0"))
                    wait_empty(pe, ("proj", "hv1"))
                    wait_empty(pe, ("level", len(LEVELS)))
                    wait_empty(pe, ("level", len(LEVELS) + 1))
                    for t, r in enumerate("AB"):
                        may_fill(pe, key, r)
                        for h in range(HH):
                            dst = ps[r][:, h * P:(h + 1) * P]
                            if t:
                                pe.matmul(dst, hattn[:, 2, h, :], hv[:, 0, h * P:(h + 1) * P], start=True, stop=False)
                            mm = pe.matmul(dst, hattn[:, t, h, :], hv[:, t, h * P:(h + 1) * P], start=(t == 0), stop=True)
                        mm.then_inc(full[r], 1)
                elif name == "hg_outT":
                    pe.wait_ge(o_done, 1)
                    for t, r in enumerate("AB"):
                        transposes(key, lambda i, t=t: hgo[:, t, i * P:(i + 1) * P], r, 8)
                elif name == "qkpT":
                    pe.wait_ge(roped, 3)
                    for t, r in enumerate("AB"):
                        may_fill(pe, key, r)
                        for i in range(4):
                            pe.transpose(ps[r][:, i * P:(i + 1) * P], qpe[:, t, i * P:(i + 1) * P], ident)
                        pe.transpose(ps[r][:, 4 * P:5 * P], kpe2[:, t, :], ident).then_inc(full[r], 1)
                elif name == "ropeT":
                    pe.wait_ge(roped, {"iq": 4, "ik": 5, "dq": 6, "dk": 7, "mq": 8, "mk": 9}[arg])
                    for t, r in enumerate("AB"):
                        if arg == "ik":
                            transposes(key, lambda i, t=t: ikr[:, t, :], r, 1)
                        else:
                            transposes(key, lambda i, t=t: ropeA[:, t, i * P:(i + 1) * P], r, 4)
                elif name == "index":
                    if arg == 0:
                        wait_empty(pe, ("ropeT", "ik"))
                    may_fill(pe, key)
                    r = region_of(key)
                    t, h0, nh = (0, 4 * arg, 4) if arg < 2 else (1, 2 * (arg - 2), 2)
                    nk = P * (t + 1)
                    for i in range(nh):
                        h = h0 + i
                        lo = 64 * (h % 2)
                        bank, at = index_at(i, nk)
                        at += 512 * bank
                        mm = pe.matmul(ps[r][:, at:at + nk], qkT["iq"][lo:lo + 64, h // 2, t * P:(t + 1) * P],
                                       ikT[lo:lo + 64, 0:nk], start=True, stop=True)
                    mm.then_inc(full[r], 1)
                elif name == "scores":
                    kind, (t, h0, nh, nb) = CHUNKS[arg]
                    if arg == 0:
                        for s in (("proj", "uq0n"), ("proj", "uq1n"), ("proj", "kn0"), ("proj", "kn1"), ("qkpT", 0)):
                            wait_empty(pe, s)
                    if arg == 3:
                        wait_empty(pe, ("ropeT", "dk"))
                    if arg == 6:
                        wait_empty(pe, ("ropeT", "mk"))
                    if arg == 9:
                        wait_empty(pe, ("proj", "xq"))
                        wait_empty(pe, ("proj", "xk"))
                    may_fill(pe, key)
                    nk = nb * P
                    for i, hl in enumerate(slots(kind, nh)):
                        h = h0 + hl
                        dst = ps["A"][:, i * nk:(i + 1) * nk]
                        tt = slice(t * P, (t + 1) * P)
                        lo = 64 * (h % 2)
                        if kind == "mla":
                            pe.matmul(dst, qn[:, h, tt], kn[:, h, 0:nk], start=True, stop=False)
                            mm = pe.matmul(dst, qpeT[lo:lo + 64, h // 2, tt], kpeT[lo:lo + 64, 0:nk], start=False, stop=True)
                        elif kind == "cross":
                            mm = pe.matmul(dst, xqT[:, h, tt], xkT[:, h, 0:nk], start=True, stop=True)
                        else:
                            q, k = (qkT["mq"], qkT["mk"]) if kind == "moba" else (qkT["dq"], qkT["dk"])
                            mm = pe.matmul(dst, q[lo:lo + 64, h // 2, tt], k[lo:lo + 64, h // 2, 0:nk], start=True, stop=True)
                    mm.then_inc(full["A"], 1)
                elif name == "probsT":
                    pe.wait_ge(probs, SEQ[arg] + 1)
                    soft_sb = soft_1 if arg < 3 else soft_2
                    transposes(key, lambda i: soft_sb[:, SEQ[arg] % 2, i * P:(i + 1) * P], "B", 8)
                elif name == "pv":
                    kind, (t, h0, nh, nb) = CHUNKS[arg]
                    may_fill(pe, key)
                    if arg == 0:
                        wait_empty(pe, ("proj", "vm0"))
                        wait_empty(pe, ("proj", "vm1"))
                    if arg == 3:
                        wait_empty(pe, ("proj", "dv"))
                    if arg == 6:
                        wait_empty(pe, ("proj", "mv"))
                    if arg == 9:
                        wait_empty(pe, ("proj", "xv"))
                    prT = (prT_1 if arg < 3 else prT_2)[:, SEQ[arg] % 2]
                    for i, hl in enumerate(slots(kind, nh)):
                        h = h0 + hl
                        for b in range(nb):
                            if kind in ("mla", "cross"):
                                v = (vm if kind == "mla" else xv)[:, b, h * P:(h + 1) * P]
                                dst = ps["B"][:, hl * P:(hl + 1) * P]
                            else:
                                v = (dv if kind == "dsa" else mv)[:, b, h * 64:(h + 1) * 64]
                                dst = ps["B"][64 * (h % 2):64 * (h % 2) + 64, (hl // 2) * P:(hl // 2 + 1) * P]
                            mm = pe.matmul(dst, v, prT[:, i * nb + b, :], start=(b == 0), stop=(b == nb - 1))
                    mm.then_inc(full["B"], 1)
                elif name == "rank":
                    pe.wait_ge(rt_mask, 1)
                    may_fill(pe, key)
                    z = ps["A"]
                    tri, one = consts[:, C_TRI:C_TRI + P], consts[:, C_ONE:C_ONE + P]
                    pe.matmul(z[:, 0:64], tri, M[:, 0, :], start=True, stop=True)
                    pe.matmul(z[:, 64:128], one, M[:, 0, :], start=True, stop=False)
                    pe.matmul(z[:, 64:128], tri, M[:, 1, :], start=False, stop=True)
                    pe.matmul(z[:, 128:192], one, M[:, 0, :], start=True, stop=False)
                    pe.matmul(z[:, 128:192], one, M[:, 1, :], start=False, stop=True).then_inc(full["A"], 1)
                elif name == "moe":
                    rounds = moe_tensor(pe)

        @block.scalar
        def _(act):
            n_seq = [0]

            def link(i):
                n_seq[0] += 1
                i.then_inc(act_seq, 1)
                act.wait_ge(act_seq, n_seq[0])

            act.dma_start(consts[:, 0:C_CAUS], ins["consts"][:, 0:C_CAUS]).then_inc(consts_in, 16)

            def col(dst, ap, k):
                act.dma_start(vec[:, dst:dst + k], ap, allow_slow_non_contiguous=True).then_inc(vec_in, 16)

            kp = "(k p) -> p k"
            act.dma_start(vec[:, V_ATT:V_ATT + 8], ins["attn_norm_w"][0].rearrange(kp, p=P),
                          allow_slow_non_contiguous=True).then_inc(att_in, 16)
            act.dma_start(consts[:, C_CAUS:], ins["consts"][:, C_CAUS:]).then_inc(masks_in, 16)
            act.dma_start(ints[:, 0:2], ins["positions"][0].rearrange("(t p) -> p t", p=P),
                          allow_slow_non_contiguous=True).then_inc(vec_in, 16)
            col(V_FFN, ins["ffn_norm_w"][0].rearrange("(p k) -> p k", k=8), 8)
            col(V_IN2, ins["g_in_2"][0].rearrange(kp, p=P), 8)
            col(V_MEM, ins["g_mem_2"][0].rearrange(kp, p=P), 8)
            col(V_HGN, ins["hg_out_norm_w"][0].rearrange(kp, p=P), 1)
            col(V_LB0, ins["hg_lower_bound"][0].rearrange(kp, p=P), 8)
            col(V_LB1, ins["hg_lower_bound"][1].rearrange(kp, p=P), 8)
            col(V_QN, ins["mla_q_norm_w"][0].rearrange(kp, p=P), 3)
            col(V_KVN, ins["mla_kv_norm_w"][0].rearrange(kp, p=P), 2)
            col(V_BM, ins["b_merge_2"][0].rearrange(kp, p=P), 24)
            act.dma_start(rbias[:, 0:8], ins["router_group_b"].broadcast_to([P, 8])).then_inc(vec_in, 16)
            act.dma_start(rbias[:, 8:72], ins["router_expert_b"].broadcast_to([P, 64])).then_inc(vec_in, 16)

            def square_sums(src, junk, n, col, width):
                for t in range(NT):
                    i = act.activation(junk(t), src(t), ACT.Square, accum_out=small[:, col + t:col + t + 1])
                    if t == NT - 1:
                        link(i)
                act.activation(small[:, col + 2:col + 4], small[:, col:col + 2], ACT.Sqrt, bias=eps,
                               scale=1.0 / width).then_inc(roots, 1)

            def evac_copy(key, dst, region=None, view=None, func=ACT.Copy, **kw):
                r = region or region_of(key)
                act.wait_ge(full[r], USE[key][r])
                act.activation(dst, view(ps[r]), func, **kw).then_inc(empty[r], 1)

            four = lambda z: z[:, :].rearrange("p (c n) -> p c n", c=4)
            rows = lambda z: z[:, :].rearrange("p (t n) -> p t n", t=2)

            for name, arg, _ in PLAN:
                key = (name, arg)
                if name == "norm":
                    if arg == "x":
                        act.wait_ge(consts_in, 16)
                        act.wait_ge(x_in, 32)
                        square_sums(lambda t: X[:, t, :], lambda t: xn[:, t, :], 0, 0, D)
                        act.wait_ge(lb_diff, 1)
                        act.activation(vec[:, V_LB:V_LB + 8], vec[:, V_LB:V_LB + 8], ACT.Sigmoid).then_inc(lb_sig, 1)
                    elif arg == "ffn":
                        wait_empty(act, ("proj", "wo0"))
                        wait_empty(act, ("proj", "wo1"))
                        square_sums(lambda t: X[:, t, :], lambda t: xnf[:, t, :], 1, 8, D)
                    elif arg == "mem":
                        act.wait_ge(mem_in, 16)
                        wait_full(act, ("scores", 2))
                        square_sums(lambda t: mem[:, t, :], lambda t: memT[:, :, :].rearrange("p k s -> p (k s)")[:, t * D:(t + 1) * D], 2, 16, D)
                elif name == "stats":
                    act.wait_ge(added, rounds * (4 * GROUPS) + 4)
                    square_sums(lambda t: X[:, t, :], lambda t: xm[:, t, :], 3, 24, D)
                    act.wait_ge(stream_scaled, 1)
                    square_sums(lambda t: X[:, t, :], lambda t: xm[:, t, :], 3, 32, D)
                elif name == "proj":
                    if arg in ("hf0", "hf1"):
                        i = int(arg[2])
                        wait_full(act, key)
                        r = region_of(key)
                        if i == 0:
                            wait_full(act, ("norm", "x"))
                        act.activation(pre[:, 4 * i:4 * i + 4, :], four(ps[r]), ACT.Sigmoid).then_inc(empty[r], 1)
                    elif arg in ("hq0", "hq1"):
                        i = int(arg[2])
                        evac_copy(key, hq[:, 4 * i:4 * i + 4, :], view=four, func=ACT.Silu)
                    elif arg in ("hv0", "hv1"):
                        i = int(arg[2])
                        evac_copy(key, hv[:, :, 512 * i:512 * i + 512], view=rows)
                    elif arg in ("hg0", "hg1"):
                        i = int(arg[2])
                        evac_copy(key, GH[:, :, 512 * i:512 * i + 512], view=rows, func=ACT.Silu)
                    elif arg == "cl":
                        evac_copy(key, C[:, :, 0:512], view=rows)
                    elif arg == "ch":
                        evac_copy(key, C[:, :, 512:704], view=lambda z: rows(z)[:, :, 0:192])
                    elif arg[:2] in ("ga", "gb"):
                        i = int(arg[2])
                        evac_copy(key, (GA if arg[1] == "a" else GB)[:, 4 * i:4 * i + 4, :], view=four, func=ACT.Sigmoid)
                    elif arg in ("uq0n", "uq1n"):
                        i = int(arg[2])
                        if i == 0:
                            wait_full(act, ("level", len(LEVELS) + 1))
                        evac_copy(key, qn[:, 4 * i:4 * i + 4, :], view=four)
                    elif arg in ("kn0", "kn1"):
                        i = int(arg[2])
                        evac_copy(key, kn[:, 4 * i:4 * i + 4, :], view=four)
                    elif arg in ("vm0", "vm1"):
                        i = int(arg[2])
                        evac_copy(key, vm[:, :, 512 * i:512 * i + 512], view=rows)
                    elif arg in ("dv", "mv"):
                        evac_copy(key, dv[:, :, :] if arg == "dv" else mv[:, :, :], view=rows)
                    elif arg in ("dg", "mg", "xg"):
                        evac_copy(key, sg[arg][:, :, :], view=four, func=ACT.Silu)
                    elif arg == "xk":
                        evac_copy(key, xkT[:, :, :], view=four)
                    elif arg == "xq":
                        evac_copy(key, xqT[:, :, :], view=four)
                    elif arg == "xv":
                        evac_copy(key, xv[:, :, :], view=rows)
                    elif arg[:2] == "gl":
                        m = int(arg[2])
                        wait_full(act, key)
                        r = region_of(key)
                        for c in range(4):
                            i = act.activation(gl[m // 2][:, 4 * (m % 2) + c, :], ps[r][:, c * S:(c + 1) * S], ACT.Sigmoid,
                                               bias=vec[:, V_BM + 4 * m + c:V_BM + 4 * m + c + 1])
                        i.then_inc(empty[r], 1)
                elif name == "cnorm":
                    wait_empty(act, ("proj", "cl"))
                    wait_empty(act, ("proj", "ch"))
                    for t in range(NT):
                        for n, (a, b) in enumerate(((0, MLA_Q), (MLA_Q, MLA_Q + MLA_KV))):
                            i = act.activation(cT[:, 0:2, :].rearrange("p a b -> p (a b)")[:, 0:b - a], C[:, t, a:b], ACT.Square,
                                               accum_out=small[:, 40 + 2 * n + t:41 + 2 * n + t])
                            link(i)
                    act.activation(small[:, 44:46], small[:, 40:42], ACT.Sqrt, bias=eps, scale=1.0 / MLA_Q)
                    act.activation(small[:, 46:48], small[:, 42:44], ACT.Sqrt, bias=eps, scale=1.0 / MLA_KV).then_inc(roots, 1)
                    act.wait_ge(angles, 1)
                    act.activation(rope1[:, :, 0:32], rope1[:, :, 32:64], ACT.Sin).then_inc(sines, 1)
                elif name == "hg_out":
                    for t, r in enumerate("AB"):
                        act.wait_ge(full[r], USE[key][r])
                        act.activation(hgsq[:, t, :], ps[r][:, :], ACT.Square).then_inc(o_sq, 1)
                    act.wait_ge(o_summed, 1)
                    act.activation(small[:, 144:160], small[:, 128:144], ACT.Sqrt, bias=eps, scale=1.0 / P).then_inc(roots, 1)
                elif name == "qkpT":
                    for t, r in enumerate("AB"):
                        act.wait_ge(full[r], USE[key][r])
                        link(act.activation(qpeT[:, :, t * P:(t + 1) * P],
                                            ps[r][:, 0:512].rearrange("p (c n) -> p c n", c=4), ACT.Copy))
                        act.activation(kpeT[:, t * P:(t + 1) * P], ps[r][:, 512:640], ACT.Copy).then_inc(empty[r], 1)
                elif name == "ropeT":
                    for t, r in enumerate("AB"):
                        act.wait_ge(full[r], USE[key][r])
                        if arg == "ik":
                            act.activation(ikT[:, t * P:(t + 1) * P], ps[r][:, 0:P], ACT.Copy).then_inc(empty[r], 1)
                        else:
                            act.activation(qkT[arg][:, :, t * P:(t + 1) * P],
                                           ps[r][:, 0:512].rearrange("p (c n) -> p c n", c=4), ACT.Copy).then_inc(empty[r], 1)
                elif name == "index":
                    if arg >= 2:
                        act.wait_ge(index_added, arg - 1)
                    evac_copy(key, relu_s[:, arg % 2, :].rearrange("p (b n) -> p b n", b=2),
                              view=lambda z: rows(z)[:, :, 0:256], func=ACT.Relu, scale=64 ** -0.5)
                elif name == "soft":
                    g = arg
                    kind, (t, h0, nh, nb) = CHUNKS[g]
                    act.wait_ge(sm_max, SEQ[g] + 1)
                    nmax, sums, _ = chunk_stats(g)
                    nk = nb * P
                    sbuf = (soft_1 if g < 3 else soft_2)[:, SEQ[g] % 2]
                    for i in range(nh):
                        x = act.activation(sbuf[:, i * nk:(i + 1) * nk], sbuf[:, i * nk:(i + 1) * nk], ACT.Exp,
                                           bias=nmax[:, i:i + 1], accum_out=sums[:, i:i + 1])
                    x.then_inc(sm_exp, 1)
                elif name == "probsT":
                    g = arg
                    if SEQ[g] >= 2:
                        wait_full(act, ("pv", AT[SEQ[g] - 2]))
                    evac_copy(key, (prT_1 if g < 3 else prT_2)[:, SEQ[g] % 2],
                              view=lambda z: z[:, :].rearrange("p (b n) -> p b n", b=8))
                elif name == "rank":
                    act.wait_ge(rt_max, 1)
                    for t in range(NT):
                        x = act.activation(lrow[:, t, :], L[:, t, 0:8], ACT.Exp, bias=small[:, 208 + t:209 + t],
                                           accum_out=small[:, 210 + t:211 + t])
                    x.then_inc(rt_exp, 1)
                    act.wait_ge(rt_max2, 1)
                    act.activation(small[:, 214:216], small[:, 212:214], ACT.Exp).then_inc(rt_exp2, 1)
                elif name == "moe":
                    rounds = moe_scalar(act)
                elif name == "final":
                    wait_empty(act, ("proj", "w20"))
                    wait_empty(act, ("proj", "w21"))
                    square_sums(lambda t: X[:, t, :], lambda t: xo[:, t, :], 4, 48, D)

        @block.vector
        def _(dve):
            n_seq = [0]

            def link(i):
                n_seq[0] += 1
                i.then_inc(dve_seq, 1)
                dve.wait_ge(dve_seq, n_seq[0])

            def tt(o, a, b, op):
                return dve.tensor_tensor(o, a, b, op)

            n_roots = [0]

            def inverse_root(col, n=2):
                n_roots[0] += 1
                dve.wait_ge(roots, n_roots[0])
                link(dve.reciprocal(small[:, col:col + n], small[:, col:col + n]))

            four = lambda z: z[:, :].rearrange("p (c n) -> p c n", c=4)
            rows = lambda z: z[:, :].rearrange("p (t n) -> p t n", t=2)

            def into_T(key, dst, wcol):
                for t, r in enumerate("AB"):
                    dve.wait_ge(full[r], USE[key][r])
                    tt(dst[:, :, t * P:(t + 1) * P], ps[r][:, :].rearrange("p (k n) -> p k n", k=KC),
                       bc(vec[:, wcol:wcol + KC], [P, KC, P], 2), ALU.mult).then_inc(empty[r], 1)

            def rope(z, heads, dst, tmp, cos, sin, release=None):
                zz = z.rearrange("p t (h d) -> p t h d", d=64)
                dd = dst.rearrange("p t (h d) -> p t h d", d=64)
                mm = tmp.rearrange("p t (h d) -> p t h d", d=64)
                shape = [P, heads, 32]
                for t in range(NT):
                    c = bc(cos[:, t, :], shape, 1)
                    s = bc(sin[:, t, :], shape, 1)
                    tt(dd[:, t, :, 0:32], zz[:, t, :, 0:32], c, ALU.mult)
                    tt(dd[:, t, :, 32:64], zz[:, t, :, 32:64], c, ALU.mult)
                    tt(mm[:, t, :, 0:32], zz[:, t, :, 32:64], s, ALU.mult)
                    x = tt(mm[:, t, :, 32:64], zz[:, t, :, 0:32], s, ALU.mult)
                if release:
                    r, n = release
                    x.then_inc(empty[r], 1)
                    dve.wait_ge(empty[r], n)
                else:
                    link(x)
                for t in range(NT):
                    tt(dd[:, t, :, 0:32], dd[:, t, :, 0:32], mm[:, t, :, 0:32], ALU.subtract)
                    x = tt(dd[:, t, :, 32:64], dd[:, t, :, 32:64], mm[:, t, :, 32:64], ALU.add)
                return x

            cos2 = consts[:, C_COS:C_COS + 64].rearrange("p (t i) -> p t i", t=2)
            sin2 = consts[:, C_SIN:C_SIN + 64].rearrange("p (t i) -> p t i", t=2)
            cos1, sin1 = rope1[:, 0:2, 0:32], rope1[:, 2:4, 0:32]

            def blocks(ap, b):
                return ap.rearrange("p h (n b) -> p (h n) b", b=2 * b)

            n_roped = [0]

            def signal_roped(i):
                n_roped[0] += 1
                i.then_inc(roped, 1)
                dve.wait_ge(roped, n_roped[0])

            for name, arg, _ in PLAN:
                key = (name, arg)
                if name == "norm" and arg == "x":
                    inverse_root(2)
                    for t in range(NT):
                        i = dve.tensor_scalar(xn[:, t, :], X[:, t, :], small[:, 2 + t:3 + t], None, ALU.mult)
                    i.then_inc(normed, 1)
                    dve.wait_ge(att_in, 16)
                    into_T(key, hT, V_ATT)
                    dve.wait_ge(vec_in, 16 * 12)
                    dve.wait_ge(masks_in, 16)
                    tt(vec[:, V_LB:V_LB + 8], vec[:, V_LB0:V_LB0 + 8], vec[:, V_LB1:V_LB1 + 8], ALU.subtract).then_inc(lb_diff, 1)
                    ang = small[:, 256:320]
                    turn = small[:, 320:384]
                    link(dve.tensor_copy(small[:, 240:242], ints[:, 0:2]))
                    for t in range(NT):
                        i = dve.tensor_scalar(ang[:, 32 * t:32 * t + 32], consts[:, C_INVF:C_INVF + 32],
                                              small[:, 240 + t:241 + t], None, ALU.mult)
                    link(i)
                    magic = 1.5 * 2.0 ** 23
                    link(dve.tensor_scalar(turn, ang, float(1 / (2 * np.pi)), None, ALU.mult))
                    link(dve.tensor_scalar(turn, turn, magic, None, ALU.add))
                    link(dve.tensor_scalar(turn, turn, -magic, None, ALU.add))
                    c1 = 6.28125
                    c2 = float(np.float32(round((2 * np.pi - c1) * 2 ** 21) / 2 ** 21))
                    c3 = 2 * np.pi - c1 - c2
                    for c in (c1, c2, c3):
                        link(dve.scalar_tensor_tensor(out=ang, in0=turn, scalar=-float(c), in1=ang, op0=ALU.mult, op1=ALU.add))
                    top = float(np.nextafter(np.float32(np.pi), np.float32(0)))
                    link(dve.tensor_scalar(turn, ang, float(np.pi / 2), None, ALU.add))
                    wrap = small[:, 384:448]
                    link(dve.tensor_scalar(wrap, turn, float(np.pi), -2 * float(np.pi), ALU.is_gt, ALU.mult))
                    link(tt(turn, turn, wrap, ALU.add))
                    dve.tensor_scalar(rope1[:, 0:2, 32:64], turn.rearrange("p (t i) -> p t i", t=2), top, -top, ALU.min, ALU.max)
                    dve.tensor_scalar(rope1[:, 2:4, 32:64], ang.rearrange("p (t i) -> p t i", t=2), top, -top,
                                      ALU.min, ALU.max).then_inc(angles, 1)
                    dve.wait_ge(lb_sig, 1)
                    link(dve.tensor_scalar(vec[:, V_OML:V_OML + 8], vec[:, V_LB:V_LB + 8], -1.0, 1.0, ALU.mult, ALU.add))
                elif name == "norm" and arg == "ffn":
                    inverse_root(10)
                    for t in range(NT):
                        i = dve.tensor_scalar(xnf[:, t, :], X[:, t, :], small[:, 10 + t:11 + t], None, ALU.mult)
                    i.then_inc(normed, 1)
                    into_T(key, hT, V_FFN)
                elif name == "norm" and arg == "mem":
                    inverse_root(18)
                    for t in range(NT):
                        i = dve.tensor_scalar(mem[:, t, :], mem[:, t, :], small[:, 18 + t:19 + t], None, ALU.mult)
                    i.then_inc(normed, 1)
                    into_T(key, memT, V_MEM)
                elif name == "stats":
                    dve.wait_ge(added, rounds * (4 * GROUPS) + 4)
                    inverse_root(26)
                    dve.wait_ge(row_in, 16)
                    for t in range(NT):
                        i = dve.scalar_tensor_tensor(out=X[:, t, :], in0=X[:, t, :], scalar=small[:, 26 + t:27 + t],
                                                     in1=wrow, op0=ALU.mult, op1=ALU.mult)
                    i.then_inc(stream_scaled, 1)
                    dve.wait_ge(stream_scaled, 1)
                    inverse_root(34)
                    for t in range(NT):
                        i = dve.tensor_scalar(xm[:, t, :], X[:, t, :], small[:, 34 + t:35 + t], None, ALU.mult)
                    i.then_inc(normed, 1)
                elif name == "norm" and arg == "mid":
                    into_T(key, hT, V_IN2)
                elif name == "proj":
                    r = region_of(key)
                    if arg in ("hq0", "hq1"):
                        i = int(arg[2])
                        wait_empty(dve, ("proj", f"hf{i}"))
                        for h in range(4 * i, 4 * i + 4):
                            x = dve.tensor_scalar(pre[:, h, :], pre[:, h, :], vec[:, V_OML + h:V_OML + h + 1],
                                                  vec[:, V_LB + h:V_LB + h + 1], ALU.mult, ALU.add)
                        link(x)
                        dve.tensor_scalar(hk[:, 4 * i:4 * i + 4, :], pre[:, 4 * i:4 * i + 4, :], -1.0, 1.0, ALU.mult, ALU.add)
                        wait_empty(dve, key)
                        x = dve.tensor_scalar(hq[:, 4 * i:4 * i + 4, :], hq[:, 4 * i:4 * i + 4, :], HG_SCALE, None, ALU.mult)
                        if i:
                            x.then_inc(hg_ready, 1)
                    elif arg in ("uq0p", "uq1p"):
                        i = int(arg[2])
                        wait_full(dve, key)
                        if i == 0:
                            dve.wait_ge(sines, 1)
                            kz = C[:, :, 640:704]
                            link(rope(kz, 1, kpe2[:, :, 0:64], kpe2[:, :, 64:128], cos1, sin1))
                            signal_roped(dve.tensor_copy(kpe2[:, :, 64:128], kpe2[:, :, 0:64]))
                        x = rope(rows(ps[r])[:, :, 0:256], 4, qpe[:, :, 256 * i:256 * i + 256],
                                 qpeT[:, :, :].rearrange("p a b -> p (a b)")[:, 0:512].rearrange("p (t n) -> p t n", t=2),
                                 cos1, sin1, (r, USE[key][r]))
                        signal_roped(x)
                    elif arg in ("wa0", "wa1"):
                        i = int(arg[2])
                        wait_full(dve, key)
                        tt(Y[:, 4 * i:4 * i + 4, :], four(ps[r]), GA[:, 4 * i:4 * i + 4, :], ALU.mult).then_inc(empty[r], 1)
                    elif arg in ("wb0", "wb1"):
                        i = int(arg[2])
                        wait_full(dve, key)
                        link(tt(GB[:, 4 * i:4 * i + 4, :], four(ps[r]), GB[:, 4 * i:4 * i + 4, :], ALU.mult))
                        tt(Y[:, 4 * i:4 * i + 4, :], Y[:, 4 * i:4 * i + 4, :], GB[:, 4 * i:4 * i + 4, :], ALU.add).then_inc(empty[r], 1)
                    elif arg in ("wo0", "wo1", "w20", "w21"):
                        i = int(arg[2])
                        wait_full(dve, key)
                        x = tt(X[:, :, 512 * i:512 * i + 512], rows(ps[r]), X[:, :, 512 * i:512 * i + 512], ALU.add)
                        x.then_inc(empty[r], 1)
                    elif arg == "rt":
                        wait_full(dve, key)
                        dve.wait_ge(vec_in, 16 * 12)
                        for t in range(NT):
                            x = tt(L[:, t, :], ps[r][:, t * 512:t * 512 + 72], rbias[:, :], ALU.add)
                        x.then_inc(empty[r], 1)
                    elif arg == "ikw":
                        wait_full(dve, key)
                        z = rows(ps[r])
                        dve.tensor_scalar(iw[:, :, :], z[:, :, 64:72], 8 ** -0.5, None, ALU.mult)
                        link(rope(z[:, :, 0:64], 1, ikr[:, :, 0:64], ikr[:, :, 64:128], cos2, sin2, (r, USE[key][r])))
                        signal_roped(dve.tensor_copy(ikr[:, :, 64:128], ikr[:, :, 0:64]))
                    elif arg in ("iq", "dq", "dk", "mq", "mk"):
                        wait_full(dve, key)
                        prev = {"dq": "iq", "dk": "dq", "mq": "dk", "mk": "mq"}.get(arg)
                        if prev:
                            wait_full(dve, ("ropeT", prev))
                        signal_roped(rope(rows(ps[r]), 8, ropeA, ropeB, cos2, sin2, (r, USE[key][r])))
                    elif arg[0] == "u" and arg[1] in "mdx":
                        i = int(arg[2])
                        wait_full(dve, key)
                        g = {"m": 0, "d": 1, "x": 2}[arg[1]]
                        part = slice(4 * i, 4 * i + 4)
                        if g == 0:
                            for n in (0, 1):
                                wait_empty(dve, ("proj", f"gl{n}"))
                            tt(gl[0][:, part, :], four(ps[r]), gl[0][:, part, :], ALU.mult).then_inc(empty[r], 1)
                        else:
                            wait_empty(dve, ("proj", f"gl{2 * g + i}"))
                            link(tt(gl[g][:, part, :], four(ps[r]), gl[g][:, part, :], ALU.mult))
                            tt(gl[0][:, part, :], gl[0][:, part, :], gl[g][:, part, :], ALU.add).then_inc(empty[r], 1)
                elif name == "level":
                    n = arg
                    if n == 0:
                        link(dve.memset(hattn[:, :, :, :], 0.0))
                    if n <= len(LEVELS):
                        mask = bc(consts[:, C_LEV + P * n:C_LEV + P * (n + 1)].bitcast(I32), [P, HH, P], 1)
                        for t, r in enumerate("AB"):
                            dve.wait_ge(full[r], USE[key][r])
                            dve.copy_predicated(hattn[:, t, :, :], mask,
                                                ps[r][:, :].rearrange("p (h n) -> p h n", h=HH)).then_inc(empty[r], 1)
                    else:
                        wait_full(dve, key)
                        dve.tensor_copy(hattn[:, 2, :, :], ps["A"][:, :].rearrange("p (h n) -> p h n", h=HH)).then_inc(empty["A"], 1)
                    if n == 0:
                        link(dve.memset(suf[:, :, :], 1.0))
                        tt(lq[:, :, :], hq[:, :, :], pre[:, :, :], ALU.mult)
                        dve.tensor_copy(lk[:, :, :], hk[:, :, :]).then_inc(hg_ready, 1)
                    elif n <= len(LEVELS):
                        b = LEVELS[n - 1]
                        bs, bp = blocks(suf, b), blocks(pre, b)
                        cnt = HH * S // (2 * b)
                        link(tt(bs[:, :, 0:b], bs[:, :, 0:b], bp[:, :, 2 * b - 1:2 * b].broadcast_to([P, cnt, b]), ALU.mult))
                        link(tt(bp[:, :, b:2 * b], bp[:, :, b:2 * b], bp[:, :, b - 1:b].broadcast_to([P, cnt, b]), ALU.mult))
                        b *= 2
                        bs, bp = blocks(suf, b), blocks(pre, b)
                        tt(blocks(lq, b)[:, :, b:2 * b], blocks(hq, b)[:, :, b:2 * b], bp[:, :, b:2 * b], ALU.mult)
                        tt(blocks(lk, b)[:, :, 0:b], blocks(hk, b)[:, :, 0:b], bs[:, :, 0:b], ALU.mult).then_inc(hg_ready, 1)
                elif name == "cnorm":
                    inverse_root(44, 4)
                    for t in range(NT):
                        dve.tensor_scalar(C[:, t, 0:MLA_Q], C[:, t, 0:MLA_Q], small[:, 44 + t:45 + t], None, ALU.mult)
                        i = dve.tensor_scalar(C[:, t, MLA_Q:640], C[:, t, MLA_Q:640], small[:, 46 + t:47 + t], None, ALU.mult)
                    i.then_inc(normed, 1)
                    for t, r in enumerate("AB"):
                        dve.wait_ge(full[r], USE[key][r])
                        tt(cT[:, :, t * P:(t + 1) * P], ps[r][:, 0:640].rearrange("p (k n) -> p k n", k=5),
                           bc(vec[:, V_QN:V_QN + 5], [P, 5, P], 2), ALU.mult).then_inc(empty[r], 1)
                elif name == "hg_out":
                    for t in range(NT):
                        dve.wait_ge(o_sq, t + 1)
                        x = dve.tensor_reduce(small[:, 128 + 8 * t:136 + 8 * t],
                                              hgsq[:, t, :].rearrange("p (h n) -> p h n", h=HH), AX.X, ALU.add)
                    x.then_inc(o_summed, 1)
                    inverse_root(144, 16)
                    for n in (0, 1):
                        wait_empty(dve, ("proj", f"hg{n}"))
                    for t, r in enumerate("AB"):
                        o3 = hgo[:, t, :].rearrange("p (h n) -> p h n", h=HH)
                        tt(o3, ps[r][:, :].rearrange("p (h n) -> p h n", h=HH),
                           bc(small[:, 144 + 8 * t:152 + 8 * t], [P, HH, P], 2), ALU.mult).then_inc(empty[r], 1)
                        dve.wait_ge(empty[r], USE[key][r])
                        x = tt(hgo[:, t, :], hgo[:, t, :], GH[:, t, :], ALU.mult)
                    x.then_inc(o_done, 1)
                elif name == "hg_outT":
                    for t, r in enumerate("AB"):
                        dve.wait_ge(full[r], USE[key][r])
                        dve.tensor_scalar(oaT[:, :, t * P:(t + 1) * P], ps[r][:, :].rearrange("p (k n) -> p k n", k=KC),
                                          vec[:, V_HGN:V_HGN + 1], None, ALU.mult).then_inc(empty[r], 1)
                elif name == "index":
                    t, h0, nh = (0, 4 * arg, 4) if arg < 2 else (1, 2 * (arg - 2), 2)
                    nk = P * (t + 1)
                    dst = score[:, 0:P] if t == 0 else score[:, P:384]
                    wait_empty(dve, key)
                    for i in range(nh):
                        bank, at = index_at(i, nk)
                        src = relu_s[:, arg % 2, 256 * bank + at:256 * bank + at + nk]
                        w = iw[:, t, h0 + i:h0 + i + 1]
                        if h0 + i == 0:
                            x = dve.tensor_scalar(dst, src, w, None, ALU.mult)
                        else:
                            x = dve.scalar_tensor_tensor(out=dst, in0=src, scalar=w, in1=dst, op0=ALU.mult, op1=ALU.add)
                        if i < nh - 1:
                            link(x)
                    x.then_inc(index_added, 1)
                    dve.wait_ge(index_added, arg + 1)
                elif name == "topk":
                    part, mask = (score[:, 0:P], dmask[:, 0:P]) if arg < 2 else (score[:, P:384], dmask[:, P:384])
                    if arg % 2 == 0:
                        own = part[:, 0:P] if arg < 2 else part[:, P:2 * P]
                        link(tt(own, own, caus, ALU.add))
                    for _ in range(TOPK // 16):
                        top = small[:, 448:456]
                        link(dve.max(top, part))
                        link(dve.match_replace(part, top, part, USED))
                    if arg % 2:
                        link(dve.tensor_scalar(mask, part, USED, NEG, ALU.not_equal, ALU.mult))
                        own = mask[:, 0:P] if arg < 2 else mask[:, P:2 * P]
                        link(tt(own, own, caus, ALU.add))
                elif name == "soft":
                    g = arg
                    kind, (t, h0, nh, nb) = CHUNKS[g]
                    nk = nb * P
                    nmax, sums, rsum = chunk_stats(g)
                    sbuf = (soft_1 if g < 3 else soft_2)[:, SEQ[g] % 2]
                    s3 = sbuf[:, 0:nh * nk].rearrange("p (h n) -> p h n", h=nh)
                    z3 = ps["A"][:, 0:nh * nk].rearrange("p (h n) -> p h n", h=nh)
                    scale = {"mla": MLA_SCALE, "dsa": 64 ** -0.5, "moba": 64 ** -0.5, "cross": 128 ** -0.5}[kind]
                    if SEQ[g] >= 2:
                        wait_full(dve, ("probsT", AT[SEQ[g] - 2]))
                    wait_full(dve, ("scores", g))
                    if g == 0:
                        wait_full(dve, ("hg_out", 0))
                    if kind == "cross":
                        x = dve.tensor_scalar(s3, z3, scale, None, ALU.mult)
                    elif kind == "dsa":
                        m = dmask[:, 0:P] if t == 0 else dmask[:, P:384]
                        x = dve.scalar_tensor_tensor(out=s3, in0=z3, scalar=scale, in1=bc(m, [P, nh, nk], 1), op0=ALU.mult, op1=ALU.add)
                    else:
                        if nb == 2:
                            dve.tensor_scalar(s3[:, :, 0:P], z3[:, :, 0:P], scale, None, ALU.mult)
                        x = dve.scalar_tensor_tensor(out=s3[:, :, nk - P:nk], in0=z3[:, :, nk - P:nk], scalar=scale,
                                                 in1=bc(caus, [P, nh, P], 1), op0=ALU.mult, op1=ALU.add)
                    x.then_inc(empty["A"], 1)
                    dve.wait_ge(empty["A"], USE["scores", g]["A"])
                    link(dve.tensor_reduce(rsum, s3, AX.X, ALU.max))
                    dve.tensor_scalar(nmax, rsum, -1.0, None, ALU.mult).then_inc(sm_max, 1)
                elif name == "normal":
                    g = arg
                    kind, (t, h0, nh, nb) = CHUNKS[g]
                    nk = nb * P
                    nmax, sums, rsum = chunk_stats(g)
                    s3 = (soft_1 if g < 3 else soft_2)[:, SEQ[g] % 2, 0:nh * nk].rearrange("p (h n) -> p h n", h=nh)
                    dve.wait_ge(sm_exp, SEQ[g] + 1)
                    link(dve.reciprocal(rsum, sums))
                    tt(s3, s3, bc(rsum, [P, nh, nk], 2), ALU.mult).then_inc(probs, 1)
                elif name == "pv":
                    g = arg
                    kind, (t, h0, nh, nb) = CHUNKS[g]
                    wait_full(dve, ("pv", g))
                    tsl = slice(t * P, (t + 1) * P)
                    if kind == "mla":
                        dve.tensor_copy(obT[:, h0:h0 + nh, tsl],
                                        ps["B"][:, 0:nh * P].rearrange("p (h n) -> p h n", h=nh)).then_inc(empty["B"], 1)
                    elif kind == "cross":
                        if t == 0:
                            wait_empty(dve, ("proj", "xg"))
                        tt(sg["xg"][:, :, tsl], ps["B"][:, 0:512].rearrange("p (h n) -> p h n", h=4),
                           sg["xg"][:, :, tsl], ALU.mult).then_inc(empty["B"], 1)
                    else:
                        gate = sg["dg" if kind == "dsa" else "mg"]
                        wait_empty(dve, ("proj", "dg" if kind == "dsa" else "mg"))
                        c0, n = h0 // 2, nh // 2
                        tt(gate[:, c0:c0 + n, tsl], ps["B"][:, 0:n * P].rearrange("p (h n) -> p h n", h=n),
                           gate[:, c0:c0 + n, tsl], ALU.mult).then_inc(empty["B"], 1)
                elif name == "rank":
                    route(dve, link, tt)
                elif name == "moe":
                    rounds = experts(dve, link, tt)
                elif name == "final":
                    wait_empty(dve, ("proj", "w20"))
                    wait_empty(dve, ("proj", "w21"))
                    inverse_root(50)
                    dve.wait_ge(row_in, 32)
                    for t in range(NT):
                        i = dve.scalar_tensor_tensor(out=xo[:, t, :], in0=X[:, t, :], scalar=small[:, 50 + t:51 + t],
                                                     in1=wrow_f, op0=ALU.mult, op1=ALU.mult)
                    i.then_inc(normed, 1)



_INS = ["x", "positions", "attn_norm_w", "w_in", "hg_lower_bound", "hg_out_norm_w", "mla_q_norm_w", "mla_w_uq",
        "mla_kv_norm_w", "mla_w_ukv", "w_branch_hgrn", "w_branch_mla", "w_out", "ffn_norm_w", "router_group_w",
        "router_group_b", "router_expert_w", "router_expert_b", "expert_w1", "expert_w3", "expert_w2",
        "final_norm_w", "mem_2", "g_in_2", "w_in_2", "b_merge_2", "g_mem_2", "w_mem_kv_2", "w_up_moba_2",
        "w_up_dsa_2", "w_up_cross_2", "w_out_2", "g_final_2"]


def kernel(**inputs):
    import concourse.bacc as bacc
    from concourse.bass_utils import run_bass_kernel_spmd

    nc = bacc.Bacc("TRN2", target_bir_lowering=False, num_devices=1)
    arrays, ins = {}, {}
    given = {name: np.ascontiguousarray(inputs[name]) for name in _INS}
    given["consts"] = shape_constants()
    for name, a in given.items():
        arrays[f"in_{name}"] = a
        ins[name] = nc.dram_tensor(f"in_{name}", a.shape, mybir.dt.from_np(a.dtype), kind="ExternalInput").ap()
    out = nc.dram_tensor("out_0", (1, S, D), F32, kind="ExternalOutput").ap()
    build(nc, ins, out)
    r = run_bass_kernel_spmd(nc, [arrays], core_ids=[0])
    return r.results[0]["out_0"]
```
